# Optimizing a Trainium2 kernel written in Bass

```python
import math
import jax, jax.numpy as jnp
from jax import lax
import numpy as np

D_MODEL = 1024
BATCH = 1
SEQ = 2048
DEPTH = 1

N_MIXERS = 2
N_SSM_LAYERS = (DEPTH + N_MIXERS - 1) // N_MIXERS
N_ATTN_LAYERS = DEPTH // N_MIXERS

SSM_EXPAND = 2
SSM_D_INNER = SSM_EXPAND * D_MODEL
SSM_HEAD_DIM = 64
SSM_HEADS = SSM_D_INNER // SSM_HEAD_DIM
SSM_STATE = 128
SSM_GROUPS = 8
SSM_HEADS_PER_GROUP = SSM_HEADS // SSM_GROUPS
SSM_CONV = 4
SSM_CHUNK = 256
SSM_CONV_DIM = SSM_D_INNER + 2 * SSM_GROUPS * SSM_STATE
SSM_IN_DIM = SSM_D_INNER + SSM_CONV_DIM + SSM_HEADS

ATTN_HEADS = 16
ATTN_HEAD_DIM = D_MODEL // ATTN_HEADS
MOBA_BLOCK = 256
MOBA_TOPK = 3
Q_BLOCK = 128

N_EXPERTS = 32
N_EXPERT_GROUPS = 4
EXPERTS_PER_GROUP = N_EXPERTS // N_EXPERT_GROUPS
TOP_K = 2
D_EXPERT = 512

DEEPNORM_ALPHA = (2.0 * DEPTH) ** 0.25
DEEPNORM_BETA = (8.0 * DEPTH) ** -0.25
LN_EPS = 1e-5
RMS_EPS = 1e-5
NEG_INF = -1e30

kernel_name = "hybrid_ssd_moba_grouped_moe_deepnorm"

def layer_norm(x, g, b):
    xf = x.astype(jnp.float32)
    mu = jnp.mean(xf, -1, keepdims=True)
    var = jnp.mean(jnp.square(xf - mu), -1, keepdims=True)
    return ((xf - mu) * lax.rsqrt(var + LN_EPS) * g + b).astype(x.dtype)

def pad_seq(h, m):
    L = h.shape[1]
    Lp = -(-L // m) * m
    return jnp.pad(h, ((0, 0), (0, Lp - L), (0, 0)))

def causal_depthwise_conv(u, w, bias):
    K = w.shape[0]
    out = lax.conv_general_dilated(u, w[:, None, :], window_strides=(1,), padding=[(K - 1, 0)],
                                   dimension_numbers=('NWC', 'WIO', 'NWC'),
                                   feature_group_count=u.shape[-1])
    return out + bias

def ssd_chunked_scan(xs, dt, a, bm, cm):
    b, Lp, G, R, P = xs.shape
    N = bm.shape[-1]
    nc = Lp // SSM_CHUNK

    def chunks(t):
        return jnp.moveaxis(t.reshape(b, nc, SSM_CHUNK, *t.shape[2:]), 1, 0)

    causal = jnp.tril(jnp.ones((SSM_CHUNK, SSM_CHUNK), dtype=bool))

    def step(state, inp):
        x_c, dt_c, b_c, c_c = inp
        acum = jnp.cumsum(dt_c * a, axis=1)
        seg = acum[:, :, None] - acum[:, None, :]
        decay = jnp.exp(jnp.where(causal[None, :, :, None, None], seg, -jnp.inf))
        w = jnp.einsum('btgn,bsgn->btsg', c_c, b_c)[..., None] * decay * dt_c[:, None]
        y = jnp.einsum('btsgr,bsgrp->btgrp', w, x_c)
        y = y + jnp.einsum('btgn,bgrpn->btgrp', c_c, state) * jnp.exp(acum)[..., None]
        to_end = jnp.exp(acum[:, -1:] - acum) * dt_c
        state = (state * jnp.exp(acum[:, -1])[..., None, None]
                 + jnp.einsum('bsgn,bsgr,bsgrp->bgrpn', b_c, to_end, x_c))
        return state, y

    state0 = jnp.zeros((b, G, R, P, N), jnp.float32)
    _, ys = lax.scan(step, state0, (chunks(xs), chunks(dt), chunks(bm), chunks(cm)))
    return jnp.moveaxis(ys, 0, 1).reshape(b, Lp, G, R, P)

def gated_group_rmsnorm(y, z, w):
    g = y * jax.nn.silu(z.astype(jnp.float32))
    gs = g.reshape(*g.shape[:-1], SSM_GROUPS, -1)
    gs = gs * lax.rsqrt(jnp.mean(gs * gs, -1, keepdims=True) + RMS_EPS)
    return gs.reshape(g.shape) * w

def mamba2_mixer(h, w_in, conv_w, conv_b, dt_bias, a_log, d_skip, norm_w, w_out):
    b, L, _ = h.shape
    hp = pad_seq(h, SSM_CHUNK)
    Lp = hp.shape[1]
    zxbcdt = hp @ w_in
    z, xbc, dt = jnp.split(zxbcdt, [SSM_D_INNER, SSM_D_INNER + SSM_CONV_DIM], axis=-1)
    xbc = jax.nn.silu(causal_depthwise_conv(xbc, conv_w, conv_b)).astype(jnp.float32)
    xs, bm, cm = jnp.split(xbc, [SSM_D_INNER, SSM_D_INNER + SSM_GROUPS * SSM_STATE], axis=-1)
    xs = xs.reshape(b, Lp, SSM_GROUPS, SSM_HEADS_PER_GROUP, SSM_HEAD_DIM)
    bm = bm.reshape(b, Lp, SSM_GROUPS, SSM_STATE)
    cm = cm.reshape(b, Lp, SSM_GROUPS, SSM_STATE)
    dt = jax.nn.softplus(dt.astype(jnp.float32) + dt_bias.astype(jnp.float32))
    dt = dt.reshape(b, Lp, SSM_GROUPS, SSM_HEADS_PER_GROUP)
    a = -jnp.exp(a_log.astype(jnp.float32)).reshape(SSM_GROUPS, SSM_HEADS_PER_GROUP)
    y = ssd_chunked_scan(xs, dt, a, bm, cm)
    y = y + d_skip.astype(jnp.float32).reshape(SSM_GROUPS, SSM_HEADS_PER_GROUP, 1) * xs
    y = gated_group_rmsnorm(y.reshape(b, Lp, SSM_D_INNER), z, norm_w.astype(jnp.float32))
    return (y.astype(h.dtype) @ w_out)[:, :L]

def moba_mixer(h, w_qkv, w_o):
    b, L, _ = h.shape
    hp = pad_seq(h, MOBA_BLOCK)
    Lp = hp.shape[1]
    nb = Lp // MOBA_BLOCK
    nqc = Lp // Q_BLOCK
    topk = min(MOBA_TOPK, nb)
    scale = ATTN_HEAD_DIM ** -0.5
    q, k, v = jnp.split(hp @ w_qkv, 3, axis=-1)

    def heads(t):
        return t.reshape(b, Lp, ATTN_HEADS, ATTN_HEAD_DIM).transpose(0, 2, 1, 3)

    q, k, v = heads(q), heads(k), heads(v)
    kb = k.reshape(b, ATTN_HEADS, nb, MOBA_BLOCK, ATTN_HEAD_DIM)
    vb = v.reshape(b, ATTN_HEADS, nb, MOBA_BLOCK, ATTN_HEAD_DIM)
    kmean = jnp.mean(kb.astype(jnp.float32), axis=3)
    qc = q.reshape(b, ATTN_HEADS, nqc, Q_BLOCK, ATTN_HEAD_DIM).transpose(0, 2, 1, 3, 4)

    def per_batch(args):
        q_b, kb_b, vb_b, km_b = args

        def per_chunk(cargs):
            q_c, ci = cargs
            q_pos = ci * Q_BLOCK + jnp.arange(Q_BLOCK)
            own = (ci * Q_BLOCK) // MOBA_BLOCK
            gate = jnp.einsum('hqd,hnd->hqn', q_c.astype(jnp.float32), km_b)
            past = jnp.arange(nb) < own
            gate = jnp.where(past[None, None, :], gate, NEG_INF)
            _, sel = lax.top_k(gate, topk)
            sel_valid = sel < own
            k_sel = jax.vmap(lambda kh, ih: kh[ih])(kb_b, sel)
            v_sel = jax.vmap(lambda vh, ih: vh[ih])(vb_b, sel)
            s_sel = jnp.einsum('hqd,hqksd->hqks', q_c, k_sel).astype(jnp.float32) * scale
            s_sel = jnp.where(sel_valid[..., None], s_sel, NEG_INF)
            s_sel = s_sel.reshape(ATTN_HEADS, Q_BLOCK, topk * MOBA_BLOCK)
            k_own = lax.dynamic_index_in_dim(kb_b, own, axis=1, keepdims=False)
            v_own = lax.dynamic_index_in_dim(vb_b, own, axis=1, keepdims=False)
            s_own = jnp.einsum('hqd,hsd->hqs', q_c, k_own).astype(jnp.float32) * scale
            k_pos = own * MOBA_BLOCK + jnp.arange(MOBA_BLOCK)
            s_own = jnp.where(k_pos[None, None, :] <= q_pos[None, :, None], s_own, NEG_INF)
            p = jax.nn.softmax(jnp.concatenate([s_sel, s_own], axis=-1), axis=-1)
            p_sel = p[..., :topk * MOBA_BLOCK].reshape(ATTN_HEADS, Q_BLOCK, topk, MOBA_BLOCK)
            p_own = p[..., topk * MOBA_BLOCK:]
            o = (jnp.einsum('hqks,hqksd->hqd', p_sel, v_sel.astype(jnp.float32))
                 + jnp.einsum('hqs,hsd->hqd', p_own, v_own.astype(jnp.float32)))
            return o.astype(h.dtype)

        return lax.map(per_chunk, (q_b, jnp.arange(nqc)))

    o = lax.map(per_batch, (qc, kb, vb, kmean))
    o = o.transpose(0, 1, 3, 2, 4).reshape(b, Lp, D_MODEL)
    return o[:, :L] @ w_o

def grouped_moe(h, w_router, b_router, w_gate, w_up, w_down):
    b, L, D = h.shape
    t = h.reshape(-1, D)
    T = t.shape[0]
    logits = (t @ w_router).astype(jnp.float32) + b_router.astype(jnp.float32)
    probs = jax.nn.softmax(logits, axis=-1)
    pg = probs.reshape(T, N_EXPERT_GROUPS, EXPERTS_PER_GROUP)
    group_score = jnp.sum(lax.top_k(pg, TOP_K)[0], axis=-1)
    g_sel = jnp.argmax(group_score, axis=-1)
    in_group = jnp.take_along_axis(pg, g_sel[:, None, None], axis=1)[:, 0]
    top_p, top_local = lax.top_k(in_group, TOP_K)
    expert_idx = g_sel[:, None] * EXPERTS_PER_GROUP + top_local
    gates = top_p / jnp.sum(top_p, axis=-1, keepdims=True)
    flat_e = expert_idx.reshape(-1)
    order = jnp.argsort(flat_e)
    tok = order // TOP_K
    xs = t[tok]
    sizes = jnp.bincount(flat_e, length=N_EXPERTS).astype(jnp.int32)
    hg = lax.ragged_dot(xs, w_gate, sizes)
    hu = lax.ragged_dot(xs, w_up, sizes)
    ye = lax.ragged_dot(jax.nn.silu(hg) * hu, w_down, sizes)
    ye = ye * gates.reshape(-1)[order][:, None].astype(ye.dtype)
    y = jax.ops.segment_sum(ye, tok, num_segments=T)
    return y.reshape(b, L, D)

def setup_inputs(seed: int = 0) -> dict:
    key = jax.random.key(seed)
    ks = jax.random.split(key, 24)
    f32 = jnp.float32
    D = D_MODEL
    nrm = lambda k, s: jax.random.normal(k, s, f32)
    x = nrm(ks[0], (BATCH, SEQ, D))
    c = nrm(ks[1], (BATCH, D))
    w_ada = nrm(ks[2], (DEPTH, D, 6 * D)) * (0.1 * D ** -0.5)
    b_ada = nrm(ks[3], (DEPTH, 6 * D)) * 0.02
    ln_g = 1.0 + 0.02 * nrm(ks[4], (DEPTH, 2, D))
    ln_b = 0.02 * nrm(ks[5], (DEPTH, 2, D))
    ssm_w_in = nrm(ks[6], (N_SSM_LAYERS, D, SSM_IN_DIM)) * D ** -0.5
    ssm_conv_w = nrm(ks[7], (N_SSM_LAYERS, SSM_CONV, SSM_CONV_DIM)) * SSM_CONV ** -0.5
    ssm_conv_b = 0.02 * nrm(ks[8], (N_SSM_LAYERS, SSM_CONV_DIM))
    dt0 = jnp.exp(jax.random.uniform(ks[9], (N_SSM_LAYERS, SSM_HEADS), f32)
                  * (math.log(0.1) - math.log(0.001)) + math.log(0.001))
    ssm_dt_bias = dt0 + jnp.log(-jnp.expm1(-dt0))
    ssm_a_log = jnp.log(jax.random.uniform(ks[10], (N_SSM_LAYERS, SSM_HEADS), f32, 1.0, 16.0))
    ssm_d = 1.0 + 0.1 * nrm(ks[11], (N_SSM_LAYERS, SSM_HEADS))
    ssm_norm_w = 1.0 + 0.02 * nrm(ks[12], (N_SSM_LAYERS, SSM_D_INNER))
    ssm_w_out = nrm(ks[13], (N_SSM_LAYERS, SSM_D_INNER, D)) * (SSM_D_INNER ** -0.5 * DEEPNORM_BETA)
    qkv_scale = jnp.concatenate([jnp.ones((2 * D,), f32), jnp.full((D,), DEEPNORM_BETA, f32)])
    attn_w_qkv = nrm(ks[14], (N_ATTN_LAYERS, D, 3 * D)) * D ** -0.5 * qkv_scale
    attn_w_o = nrm(ks[15], (N_ATTN_LAYERS, D, D)) * (D ** -0.5 * DEEPNORM_BETA)
    w_router = nrm(ks[16], (D, N_EXPERTS)) * D ** -0.5
    b_router = 0.01 * nrm(ks[17], (N_EXPERTS,))
    moe_w_gate = nrm(ks[18], (DEPTH, N_EXPERTS, D, D_EXPERT)) * D ** -0.5
    moe_w_up = nrm(ks[19], (DEPTH, N_EXPERTS, D, D_EXPERT)) * D ** -0.5
    moe_w_down = nrm(ks[20], (DEPTH, N_EXPERTS, D_EXPERT, D)) * (D_EXPERT ** -0.5 * DEEPNORM_BETA)
    return {"x": x, "c": c, "w_ada": w_ada, "b_ada": b_ada, "ln_g": ln_g, "ln_b": ln_b,
            "ssm_w_in": ssm_w_in, "ssm_conv_w": ssm_conv_w, "ssm_conv_b": ssm_conv_b,
            "ssm_dt_bias": ssm_dt_bias, "ssm_a_log": ssm_a_log, "ssm_d": ssm_d,
            "ssm_norm_w": ssm_norm_w, "ssm_w_out": ssm_w_out,
            "attn_w_qkv": attn_w_qkv, "attn_w_o": attn_w_o,
            "w_router": w_router, "b_router": b_router,
            "moe_w_gate": moe_w_gate, "moe_w_up": moe_w_up, "moe_w_down": moe_w_down}

def reference(x, c, w_ada, b_ada, ln_g, ln_b, ssm_w_in, ssm_conv_w, ssm_conv_b, ssm_dt_bias,
              ssm_a_log, ssm_d, ssm_norm_w, ssm_w_out, attn_w_qkv, attn_w_o, w_router, b_router,
              moe_w_gate, moe_w_up, moe_w_down):
    cs = jax.nn.silu(c)
    for i in range(DEPTH):
        mod = cs @ w_ada[i] + b_ada[i]
        sh1, sc1, g1, sh2, sc2, g2 = jnp.split(mod, 6, axis=-1)
        hm = x * (1.0 + sc1[:, None]) + sh1[:, None]
        j = i // N_MIXERS
        if i % N_MIXERS == 0:
            y = mamba2_mixer(hm, ssm_w_in[j], ssm_conv_w[j], ssm_conv_b[j], ssm_dt_bias[j],
                             ssm_a_log[j], ssm_d[j], ssm_norm_w[j], ssm_w_out[j])
        else:
            y = moba_mixer(hm, attn_w_qkv[j], attn_w_o[j])
        x = layer_norm(DEEPNORM_ALPHA * x + (1.0 + g1[:, None]) * y, ln_g[i, 0], ln_b[i, 0])
        hm = x * (1.0 + sc2[:, None]) + sh2[:, None]
        y = grouped_moe(hm, w_router, b_router, moe_w_gate[i], moe_w_up[i], moe_w_down[i])
        x = layer_norm(DEEPNORM_ALPHA * x + (1.0 + g2[:, None]) * y, ln_g[i, 1], ln_b[i, 1])
    return x


_drawn_inputs = setup_inputs


def setup_inputs(seed=0):
    import zlib

    import numpy as np

    out = dict(_drawn_inputs(seed))
    spreads = {}
    factors = {}
    for name, (base, spread) in spreads.items():
        noise = np.random.default_rng([zlib.crc32(name.encode()), seed]).standard_normal(out[name].shape)
        drawn = base * np.exp(spread * noise) if base else spread * noise
        out[name] = __import__('jax').numpy.asarray(drawn.astype(out[name].dtype))
    for name, factor in factors.items():
        out[name] = (out[name] * factor).astype(out[name].dtype)
    return out
```

```python
from contextlib import ExitStack

import concourse.bass as bass
from concourse import mybir

F32 = mybir.dt.float32
F32R = mybir.dt.float32r
I32 = mybir.dt.int32
ALU = mybir.AluOpType
ACT = mybir.ActivationFunctionType
AX = mybir.AxisListType

P = 128
D = 1024
SEQ = 2048
KK = D // P
TT = SEQ // P
DI = 2048
GROUPS = 8
STATE = 128
HEADS = 32
RH = HEADS // GROUPS
HD = 64
GW = RH * HD
CHUNK = 256
NC_ = SEQ // CHUNK
STEPS = GROUPS * NC_
XBC = DI
COL_B = XBC + DI
COL_C = COL_B + GROUPS * STATE
COL_DT = COL_C + GROUPS * STATE
TAPS = 4
CONV = 4
PARTS = CONV + 1
EXPERTS = 32
EGROUPS = 4
EPG = EXPERTS // EGROUPS
FE = 512
ALPHA = 2.0 ** 0.25
EPS = 1e-5
MAXT = 64
YTILES = DI // P


def in_loop(i, low=0, high=STEPS):
    return not isinstance(i, int) or low <= i < high


def constants(nc, k):
    block = k.ctx1.enter_context(nc.Block())

    @block.gpsimd
    def _(pool):
        nc.gpsimd.memset(k.ident[:], 0.0).then_inc(k.const_set, 1)
        nc.gpsimd.memset(k.ones[:], 1.0).then_inc(k.const_set, 1)
        nc.gpsimd.memset(k.mask3[:], 1.0).then_inc(k.const_set, 1)
        nc.gpsimd.memset(k.below[:], 1.0).then_inc(k.const_set, 1)
        nc.gpsimd.memset(k.keep[:], 1.0).then_inc(k.const_set, 1)
        nc.gpsimd.memset(k.negh[:], -0.5).then_inc(k.const_set, 1)
        nc.gpsimd.iota(k.eidx_i[:], pattern=[[1, EPG]], base=0, channel_multiplier=0).then_inc(k.const_set, 1)
        nc.gpsimd.iota(k.tidx_i[:], pattern=[[1, MAXT]], base=0, channel_multiplier=0).then_inc(k.const_set, 1)
        nc.gpsimd.iota(k.tok_i[:], pattern=[[P, TT]], base=0, channel_multiplier=1).then_inc(k.const_set, 1)
        nc.gpsimd.memset(k.eps[:], EPS).then_inc(k.const_set, 1)
        pool.wait_ge(k.const_set, 10)
        nc.gpsimd.affine_select(out=k.ident[:], in_=k.ident[:], compare_op=ALU.not_equal, fill=1.0, base=0,
                                pattern=[[-1, P]], channel_multiplier=1).then_inc(k.const_set, 1)
        for q in (0, 2):
            nc.gpsimd.affine_select(out=k.mask3[:, q * P:(q + 1) * P], in_=k.mask3[:, q * P:(q + 1) * P],
                                    compare_op=ALU.is_ge, fill=0.0, base=0, pattern=[[1, P]],
                                    channel_multiplier=-1).then_inc(k.const_set, 1)
        nc.gpsimd.affine_select(out=k.below[:], in_=k.below[:], compare_op=ALU.is_gt, fill=0.0, base=0,
                                pattern=[[1, P]], channel_multiplier=-1).then_inc(k.const_set, 1)
        nc.gpsimd.memset(k.keep[:, 0:STEPS + 1:NC_], 0.0).then_inc(k.const_set, 1)
        nc.gpsimd.tensor_copy(k.eidx[:], k.eidx_i[:]).then_inc(k.const_set, 1)
        nc.gpsimd.tensor_copy(k.tidx[:], k.tidx_i[:]).then_inc(k.const_set, 1)
        nc.gpsimd.tensor_copy(k.tok[:], k.tok_i[:]).then_inc(k.const_set, 1)
        pool.wait_ge(k.const_set, 18)


def clear_semaphores(nc, k):
    with nc.Block() as block:

        @block.gpsimd
        def _(pool):
            for s in k.used:
                pool.sem_clear(s)


def stage(nc, k, build, *args):
    with ExitStack() as semaphores:
        k.used, k.semaphores = [], semaphores
        build(nc, k, *args)
        clear_semaphores(nc, k)


def modulated_input(nc, k):
    with ExitStack() as ctx:
        sb, ps, sem = k.makers(ctx)
        NS = 4
        wa = [sb(f"wa{s}", [P, KK, 512], F32) for s in range(NS)]
        xt = [sb(f"xt{s}", [P, D], F32) for s in range(8)]
        hf = [sb(f"hf{s}", [P, KK, 512], F32) for s in range(2)]
        hl = sb("hl", [P, 2, 2, KK, CHUNK], F32R)
        c_in = sb("c_in", [P, KK], F32)
        c_th = sb("c_th", [P, KK], F32)
        c_half = sb("c_half", [P, KK], F32)
        bcol = sb("bcol", [P, 16], F32)
        mcol = sb("mcol", [P, 16], F32)
        wdt = sb("wdt", [P, KK, HEADS], F32)
        dtb = sb("dtb", [P, HEADS], F32)
        al = sb("al", [P, HEADS], F32)
        v = sb("v", [P, TT * HEADS], F32)
        nv = sb("nv", [P, TT * HEADS], F32)
        e = sb("e", [P, TT * HEADS], F32)
        u = sb("u", [P, TT * HEADS], F32)
        ln = sb("ln", [P, TT * HEADS], F32)
        zr = sb("zr", [P, TT * HEADS], F32)
        dtn = sb("dtn", [P, TT * HEADS], F32)
        dta = sb("dta", [P, TT * HEADS], F32)
        acrow = sb("acrow", [P, 4, P], F32)
        adaP = ps("adaP", [P, 512])
        dtP = ps("dtP", [P, 512])
        acP = ps("acP", [P, 512])
        rowP = ps("rowP", [P, 512])
        trP = [ps(f"trP{s}", [P, 512]) for s in range(4)]
        small_in, c_act, cs_ready = sem("small_in"), sem("c_act"), sem("cs_ready")
        wa_in = [sem(f"wa_in{s}") for s in range(NS)]
        x_in = [sem(f"x_in{s}") for s in range(8)]
        ada_mm, mcol_ready = sem("ada_mm"), sem("mcol_ready")
        tr_done, full_ready, hi_ready, lo_ready = (sem(n) for n in ("tr_done", "full_ready", "hi_ready", "lo_ready"))
        hm_out, dt_mm, chain, act_chain, ac_mm = (sem(n) for n in ("hm_out", "dt_mm", "chain", "act_chain", "ac_mm"))
        ac_tr, row_ready, row_out, x_used = sem("ac_tr"), sem("row_ready"), sem("row_out"), sem("x_used")
        par_done = sem("par_done")
        block = ctx.enter_context(nc.Block())
        w_ada = k.d["w_ada"].rearrange("(kk p) n -> p kk n", p=P)

        @block.sync
        def _(sp):
            sp.dma_start(c_in[:], k.d["c_cols"]).then_inc(small_in, 16)
            sp.dma_start(bcol[:], k.d["b_ada_cols"]).then_inc(small_in, 16)
            sp.dma_start(k.par[:], k.d["conv_par"]).then_inc(small_in, 16)
            sp.dma_start(dtb[:], k.d["dt_bias"].partition_broadcast(P)).then_inc(small_in, 16)
            sp.dma_start(al[:], k.d["a_log"].partition_broadcast(P)).then_inc(small_in, 16)
            sp.dma_start(k.drow[:], k.d["d_skip"].partition_broadcast(P)).then_inc(small_in, 16)
            sp.dma_start(k.nwrow[:], k.d["norm_w"].partition_broadcast(P)).then_inc(small_in, 16)
            sp.dma_start(wdt[:], k.d["w_in"].rearrange("(kk p) n -> p kk n", p=P)[:, :, COL_DT:COL_DT + HEADS]
                         ).then_inc(small_in, 16)
            for s in range(NS):
                sp.dma_start(wa[s][:], w_ada[:, :, s * 512:(s + 1) * 512]).then_inc(wa_in[s], 16)
            with sp.Fori(0, 4) as tb:
                for q in range(2):
                    sp.wait_ge(lo_ready, KK * (tb + 1))
                    sp.dma_start(k.hmd[bass.ds(2 * tb + q, 1)].rearrange("a p n -> (a p) n"),
                                 hl[:, q].rearrange("p s k t -> p (s k t)").bitcast(F32)).then_inc(hm_out, 16)
            sp.wait_ge(hm_out, 16 * 8)
            sp.wait_ge(row_ready, 1)
            sp.dma_start(k.acd.rearrange("(q h) t -> h q t", h=P), acrow[:]).then_inc(row_out, 16)
            sp.wait_ge(row_out, 16)

        @block.scalar
        def _(act):
            for t in range(8):
                act.dma_start(xt[t][:], k.d["x"][t * P:(t + 1) * P, :]).then_inc(x_in[t], 16)
            act.wait_ge(small_in, 16 * 8)
            nc.scalar.activation(c_th[:], c_in[:], ACT.Tanh, scale=0.5).then_inc(c_act, 1)

            def block_of_tokens(tb, q):
                for kk in range(KK):
                    act.wait_ge(full_ready, KK * (tb + q) + kk + 1)
                    if kk == 0 and in_loop(tb + q, 1):
                        act.wait_ge(hm_out, 32 * (tb + q))
                    nc.scalar.copy(hl[:, :, 0, kk, :], hf[q][:, kk, :].rearrange("p (c t) -> p c t", c=2)
                                   ).then_inc(hi_ready, 1)

            block_of_tokens(0, 0)
            for t in range(8):
                act.wait_ge(x_used, t // 4 + 1)
                act.dma_start(xt[t][:], k.d["x"][(8 + t) * P:(9 + t) * P, :]).then_inc(x_in[t], 16)
                if t == 3:
                    block_of_tokens(0, 1)
            block_of_tokens(2, 0)
            block_of_tokens(2, 1)
            act.wait_ge(chain, 5)
            nc.scalar.activation(e[:], nv[:], ACT.Exp).then_inc(act_chain, 1)
            nc.scalar.activation(al[:], al[:], ACT.Exp).then_inc(act_chain, 1)
            act.wait_ge(chain, 6)
            nc.scalar.activation(ln[:], u[:], ACT.Ln).then_inc(act_chain, 1)
            act.wait_ge(chain, 16)
            nc.scalar.activation(k.tab[:, 2, :], k.tab[:, 1, :], ACT.Exp).then_inc(act_chain, 1)
            act.wait_ge(ac_tr, 1)
            nc.scalar.copy(acrow[:].rearrange("p q t -> p (q t)"), rowP[:]).then_inc(row_ready, 1)

        @block.tensor
        def _(pe):
            pe.wait_ge(cs_ready, 1)
            for s in range(NS):
                pe.wait_ge(wa_in[s], 16)
                for j in range(4):
                    for kk in range(KK):
                        mm = nc.tensor.matmul(adaP[:, s * 4 + j:s * 4 + j + 1], wa[s][:, kk, j * P:(j + 1) * P],
                                              k.cs[:, kk:kk + 1], start=kk == 0, stop=kk == KK - 1)
            mm.then_inc(ada_mm, 1)

            def block_of_tokens(tb, q):
                for j in range(4):
                    pe.wait_ge(x_in[4 * q + j], 8 * tb + 16)
                for kk in range(KK):
                    if kk >= 4 or in_loop(tb + q, 1):
                        pe.wait_ge(full_ready, KK * (tb + q) + kk - 3)
                    for j in range(4):
                        tr = nc.tensor.transpose(trP[kk % 4][:, j * P:(j + 1) * P],
                                                 xt[4 * q + j][:, kk * P:(kk + 1) * P], k.ident[:])
                    tr.then_inc(tr_done, 1)
                    if kk == KK - 1:
                        pe.wait_ge(tr_done, KK * (tb + q) + KK)
                        pe.sem_inc(x_used, 1)
                pe.wait_ge(full_ready, KK * (tb + q) + KK)
                for j in range(4):
                    for kk in range(KK):
                        mm = nc.tensor.matmul(dtP[:, ((tb + q) * 4 + j) * HEADS:((tb + q) * 4 + j + 1) * HEADS],
                                              hf[q][:, kk, j * P:(j + 1) * P], wdt[:, kk, :],
                                              start=kk == 0, stop=kk == KK - 1)
                mm.then_inc(dt_mm, 1)

            for t in range(4):
                block_of_tokens(2 * (t // 2), t % 2)
            pe.wait_ge(chain, 14)
            nc.tensor.matmul(acP[:], k.mask3[:, 0:P], dta[:], start=True, stop=False, skip_group_check=True)
            nc.tensor.matmul(acP[:].rearrange("p (c a h) -> p a c h", c=NC_, a=2)[:, 1], k.ones[:, 0:P],
                             dta[:].rearrange("p (c a h) -> p a c h", c=NC_, a=2)[:, 0],
                             start=False, stop=True, skip_group_check=True).then_inc(ac_mm, 1)
            pe.wait_ge(chain, 16)
            for q in range(4):
                tr = nc.tensor.transpose(rowP[:, q * P:(q + 1) * P], k.tab[:, 1, q * P:(q + 1) * P], k.ident[:])
            tr.then_inc(ac_tr, 1)

        @block.vector
        def _(dve):
            count = [0]

            def link(ins):
                count[0] += 1
                ins.then_inc(chain, 1)
                dve.wait_ge(chain, count[0])

            dve.wait_ge(small_in, 16 * 8)
            nc.vector.tensor_scalar(k.par[:], k.par[:], 0.5, None, ALU.mult).then_inc(par_done, 1)
            nc.vector.tensor_scalar(k.nwrow[:], k.nwrow[:], 0.5, None, ALU.mult).then_inc(par_done, 1)
            link(nc.vector.tensor_scalar(c_half[:], c_in[:], 0.5, None, ALU.mult))
            dve.wait_ge(c_act, 1)
            nc.vector.scalar_tensor_tensor(out=k.cs[:], in0=c_th[:], scalar=1.0, in1=c_half[:], op0=ALU.add,
                                           op1=ALU.mult).then_inc(cs_ready, 1)
            dve.wait_ge(ada_mm, 1)
            link(nc.vector.tensor_tensor(mcol[:], adaP[:, 0:16], bcol[:], ALU.add))
            link(nc.vector.tensor_scalar(mcol[:, 8:16], mcol[:, 8:16], 1.0, None, ALU.add))

            def block_of_tokens(tb, q):
                if in_loop(tb + q, 2):
                    dve.wait_ge(dt_mm, tb + q - 1)
                    dve.wait_ge(hi_ready, KK * (tb + q - 1))
                for kk in range(KK):
                    dve.wait_ge(tr_done, KK * (tb + q) + kk + 1)
                    nc.vector.tensor_scalar(hf[q][:, kk, :], trP[kk % 4][:], mcol[:, 8 + kk:9 + kk],
                                            mcol[:, kk:kk + 1], ALU.mult, ALU.add).then_inc(full_ready, 1)
                    if kk >= 1:
                        low_part(tb, q, kk - 1)
                low_part(tb, q, KK - 1)

            def low_part(tb, q, kk):
                dve.wait_ge(full_ready, KK * (tb + q) + kk + 1)
                dve.wait_ge(hi_ready, KK * (tb + q) + kk + 1)
                nc.vector.tensor_tensor(hl[:, :, 1, kk, :], hf[q][:, kk, :].rearrange("p (c t) -> p c t", c=2),
                                        hl[:, :, 0, kk, :].bitcast(F32), ALU.subtract).then_inc(lo_ready, 1)

            for t in range(4):
                block_of_tokens(2 * (t // 2), t % 2)
            dve.wait_ge(dt_mm, 4)
            vh = v[:].rearrange("p (t h) -> p t h", h=HEADS)
            link(nc.vector.tensor_tensor(vh, dtP[:].rearrange("p (t h) -> p t h", h=HEADS),
                                         dtb[:].unsqueeze(1).to_broadcast([P, TT, HEADS]), ALU.add))
            link(nc.vector.scalar_tensor_tensor(out=nv[:], in0=v[:], scalar=-1.0, in1=v[:], op0=ALU.mult, op1=ALU.min))
            dve.wait_ge(act_chain, 1)
            link(nc.vector.tensor_scalar(u[:], e[:], 1.0, None, ALU.add))
            link(nc.vector.tensor_scalar(nv[:], u[:], -1.0, None, ALU.add))
            link(nc.vector.tensor_scalar(zr[:], nv[:], 0.0, None, ALU.is_equal))
            link(nc.vector.tensor_scalar(nv[:], nv[:], 1e-30, None, ALU.max))
            link(nc.vector.reciprocal(nv[:], nv[:]))
            dve.wait_ge(act_chain, 3)
            link(nc.vector.tensor_tensor(nv[:], nv[:], ln[:], ALU.mult))
            link(nc.vector.tensor_tensor(nv[:], nv[:], zr[:], ALU.add))
            link(nc.vector.tensor_tensor(nv[:], nv[:], e[:], ALU.mult))
            dtg = "p (c a g r) -> p a c g r"
            tabg = "p (g c a r) -> p a c g r"
            n = count[0]
            nc.vector.scalar_tensor_tensor(out=dtn[:], in0=v[:], scalar=0.0, in1=nv[:], op0=ALU.max,
                                           op1=ALU.add).then_inc(par_done, 1)
            dve.wait_ge(par_done, 3)
            nc.vector.scalar_tensor_tensor(out=dta[:].rearrange("p (t h) -> p t h", h=HEADS),
                                           in0=dtn[:].rearrange("p (t h) -> p t h", h=HEADS), scalar=-1.0,
                                           in1=al[:].unsqueeze(1).to_broadcast([P, TT, HEADS]), op0=ALU.mult,
                                           op1=ALU.mult).then_inc(chain, 14 - n)
            count[0] = 14
            for a in range(2):
                nc.vector.tensor_copy(k.tab[:, 0, :].rearrange(tabg, g=GROUPS, c=NC_, a=2)[:, a],
                                      dtn[:].rearrange(dtg, c=NC_, a=2, g=GROUPS)[:, a]).then_inc(par_done, 1)
            dve.wait_ge(ac_mm, 1)
            for a in range(2):
                nc.vector.tensor_copy(k.tab[:, 1, :].rearrange(tabg, g=GROUPS, c=NC_, a=2)[:, a],
                                      acP[:].rearrange(dtg, c=NC_, a=2, g=GROUPS)[:, a]).then_inc(chain, 1)
            dve.wait_ge(chain, 16)
            dve.wait_ge(act_chain, 4)


def by_group(eng, step):
    for c in range(NC_):
        step(c, c % 2, last=c == NC_ - 1)
    with eng.Fori(1, GROUPS - 1) as g:
        step(NC_ * g, 0, first=True)
        step(NC_ * g + 1, 1)
        with eng.Fori(1, NC_ // 2 - 1) as h:
            step(NC_ * g + 2 * h, 0)
            step(NC_ * g + 2 * h + 1, 1)
        step(NC_ * g + NC_ - 2, 0)
        step(NC_ * g + NC_ - 1, 1, last=True)
    start = NC_ * (GROUPS - 1)
    step(start, 0, first=True)
    step(start + 1, 1)
    with eng.Fori(1, NC_ // 2) as h:
        step(start + 2 * h, 0)
        step(start + 2 * h + 1, 1)
    step(STEPS, 0)
    step(STEPS + 1, 1)


def mixer_steps(nc, k):
    with ExitStack() as ctx:
        sb, ps, sem = k.makers(ctx)
        wide = [P] * CONV + [GW]
        w_raw = [sb(f"w_raw{m}", [P, KK, wide[m]]) for m in range(PARTS)]
        w_hi = [sb(f"w_hi{m}", [P, KK, wide[m]], F32R) for m in range(PARTS)]
        w_lo = [sb(f"w_lo{m}", [P, KK, wide[m]], F32R) for m in range(PARTS)]
        hm = [sb(f"hm{b}", [P, 2, KK, CHUNK], F32R) for b in range(2)]
        zero = sb("zero_rows", [P, CHUNK])
        zero_set, zero_out = sem("zero_set"), sem("zero_out")
        acb = [sb(f"acb{b}", [P, 2, RH, P]) for b in range(2)]
        parb = [sb(f"parb{b}", [P, CONV, TAPS + 1]) for b in range(2)]
        tb = [sb(f"tb{b}", [P, 3, 2, RH]) for b in range(2)]
        ub = [sb(f"ub{b}", [P, CONV, CHUNK + TAPS - 1]) for b in range(2)]
        cv = [sb(f"cv{b}", [P, CONV, CHUNK]) for b in range(2)]
        th = sb("th", [P, CONV, CHUNK])
        xbc = [sb(f"xbc{b}", [P, CONV, CHUNK]) for b in range(2)]
        xs = sb("xs", [P, 2, GW])
        bs = sb("bs", [P, 2, P])
        zth = sb("zth", [P, 2, GW])
        zs = [sb(f"zs{b}", [P, 2, GW]) for b in range(2)]
        seg0, seg1 = sb("seg0", [P, RH, CHUNK]), sb("seg1", [P, RH, P])
        gm = sb("gm", [P, 3 * P])
        wt0, wt1 = sb("wt0", [P, RH, CHUNK]), sb("wt1", [P, RH, P])
        te = sb("te", [P, 2, RH])
        el = sb("el", [P, RH])
        ek = sb("ek", [P, RH])
        xdt, xend, xd = (sb(n, [P, 2, GW]) for n in ("xdt", "xend", "xd"))
        st, stt = sb("st", [P, GW]), sb("stt", [P, GW])
        t1, y, gt, gw, yn = (sb(n, [P, 2, GW]) for n in ("t1", "y", "gt", "gw", "yn"))
        sq = sb("sq", [P, 2, GW])
        ss, ms, rs = sb("ss", [P, 2]), sb("ms", [P, 2]), sb("rs", [P, 2])
        yt = [sb(f"yt{b}", [P, 2, 2, P]) for b in range(2)]
        pj = [ps(f"pj{b}", [P, 512]) for b in range(3)]
        tx, gp, yi, yx, sbp = (ps(n, [P, 512]) for n in ("tx", "gp", "yi", "yx", "sbp"))

        w_in_s = [sem(f"w_in_s{m}") for m in range(PARTS)]
        w_hi_s = sem("w_hi_s")
        w_split = [sem(f"w_split{m}") for m in range(PARTS)]
        hm_in = [sem(f"hm_in{b}") for b in range(2)]
        ac_in = [sem(f"ac_in{b}") for b in range(2)]
        y_stored = [sem(f"y_stored{b}") for b in range(2)]
        (proj_done, conv_out, z_out, par_ready, halo_done, conv_tap, th_done, silu_done, xs_tr, b_tr, g_done,
         xs_out, b_out, zth_done, seg_done, exp_done, el_done, te_done, ek_done, gm_done, w_done,
         x_done, y_mm, st_mm, stt_done, st_done, t1_done, y_done, y3_done, gt_done, gw_done, sq_done, ms_done,
         rs_done, yn_done, yt_tr, yt_out, ub_out) = (sem(n) for n in (
             "proj_done conv_out z_out par_ready halo_done conv_tap th_done silu_done xs_tr b_tr g_done "
             "xs_out b_out zth_done seg_done exp_done el_done te_done ek_done gm_done w_done "
             "x_done y_mm st_mm stt_done st_done t1_done y_done y3_done gt_done gw_done sq_done ms_done "
             "rs_done yn_done yt_tr yt_out ub_out").split())
        block = ctx.enter_context(nc.Block())
        w_cols = k.d["w_in"].rearrange("(kk p) n -> p kk n", p=P)

        @block.sync
        def _(sp):
            def weights(g):
                for m, (base, width) in enumerate(((XBC, GW), (XBC + P, GW), (COL_B, STATE), (COL_C, STATE),
                                                   (0, GW))):
                    if in_loop(g, 1, GROUPS):
                        sp.wait_ge(w_split[m], g)
                        sp.sem_inc(k.passed, 1)
                    sp.dma_start(w_raw[m][:], w_cols[:, :, bass.ds(g * width + base, wide[m])]
                                 ).then_inc(w_in_s[m], 16)

            def step(i, b):
                if in_loop(i, 2):
                    sp.wait_ge(proj_done, 6 * (i - 1))
                sp.dma_start(hm[b][:].rearrange("p s k t -> p (s k t)").bitcast(F32),
                             k.hmd[bass.ds(i % NC_, 1)]
                             .rearrange("a p n -> (a p) n")).then_inc(hm_in[b], 16)
                if in_loop(i, 2):
                    sp.wait_ge(seg_done, 8 * (i - 1))
                    sp.wait_ge(el_done, i - 1)
                sp.dma_start(acb[b][:].rearrange("p a r t -> p (a r t)"),
                             k.acd.rearrange("(i n) t -> i (n t)", i=STEPS)[bass.ds(i, 1), :]
                             .rearrange("a n -> (a n)").partition_broadcast(P)).then_inc(ac_in[b], 16)

            def clear(g):
                n = MAXT // 2 // GROUPS
                sp.dma_start(k.ysd[bass.ds((MAXT // 2 + n * g) * P, n * P), :]
                             .rearrange("(p t) (q n) -> p (t q) n", p=P, n=CHUNK),
                             zero[:].unsqueeze(1).to_broadcast([P, n * D // CHUNK, CHUNK])).then_inc(zero_out, 16)

            weights(0)
            for c in range(4):
                step(c, c % 2)
            weights(1)
            sp.wait_ge(zero_set, 1)
            clear(0)
            for c in range(4, 8):
                step(c, c % 2)
            with sp.Fori(1, GROUPS - 1) as g:
                for c in range(4):
                    step(g * NC_ + c, c % 2)
                weights(g + 1)
                clear(g)
                for c in range(4, 8):
                    step(g * NC_ + c, c % 2)
            clear(GROUPS - 1)
            for c in range(8):
                step(8 * (GROUPS - 1) + c, c % 2)
            sp.wait_ge(zero_out, 16 * GROUPS)

        @block.gpsimd
        def _(pool):
            def x_products(j):
                xsv = xs[:].rearrange("p a (r q) -> p (a r) q", r=RH)
                pool.wait_ge(xs_out, j + 1)
                if in_loop(j, 1):
                    pool.wait_ge(st_mm, j)
                return xsv

            def tasks(j, b):
                if in_loop(j, 1):
                    gate(j - 1, 1 - b)
                xsv = x_products(j)
                nc.gpsimd.tensor_tensor(xdt[:].rearrange("p a (r q) -> p (a r) q", r=RH), xsv,
                                        tb[b][:, 0].rearrange("p a r -> p (a r)").unsqueeze(2)
                                        .to_broadcast([P, 2 * RH, HD]), ALU.mult).then_inc(x_done, 1)
                for a in range(2):
                    ins = nc.gpsimd.tensor_tensor(
                        xd[:, a].rearrange("p (r q) -> p r q", r=RH), xs[:, a].rearrange("p (r q) -> p r q", r=RH),
                        k.drow[:, bass.ds(RH * (j // NC_), RH)].unsqueeze(2).to_broadcast([P, RH, HD]),
                        ALU.mult)
                    ins.then_inc(x_done, 1)
                pool.wait_ge(te_done, 2 * (j + 1))
                nc.gpsimd.tensor_tensor(xend[:].rearrange("p a (r q) -> p (a r) q", r=RH), xsv,
                                        te[:].rearrange("p a r -> p (a r)").unsqueeze(2)
                                        .to_broadcast([P, 2 * RH, HD]), ALU.mult).then_inc(x_done, 1)

            def gate(j, b):
                pool.wait_ge(y_done, j + 1)
                pool.wait_ge(x_done, 4 * j + 3)
                nc.gpsimd.tensor_tensor(xd[:], y[:], xd[:], ALU.add).then_inc(y3_done, 1)
                pool.wait_ge(y3_done, j + 1)
                pool.wait_ge(z_out, 2 * (j + 1))
                if in_loop(j, 1):
                    pool.wait_ge(sq_done, 2 * j)
                nc.gpsimd.tensor_tensor(gt[:], xd[:], zs[b][:], ALU.mult).then_inc(gt_done, 1)
                pool.wait_ge(gt_done, j + 1)
                if in_loop(j, 1):
                    pool.wait_ge(yn_done, 2 * j)
                for a in range(2):
                    nc.gpsimd.tensor_tensor(gw[:, a], gt[:, a],
                                            k.nwrow[:, bass.ds(GW * (j // NC_), GW)], ALU.mult
                                            ).then_inc(gw_done, 1)
                pool.wait_ge(sq_done, 2 * (j + 1))
                nc.gpsimd.tensor_tensor(ms[:], ss[:], k.eps[:], ALU.add).then_inc(ms_done, 1)
                pool.wait_ge(ms_done, j + 1)
                nc.gpsimd.tensor_tensor(rs[:], ms[:], k.negh[:], ALU.pow).then_inc(rs_done, 1)

            nc.gpsimd.memset(zero[:], 0.0).then_inc(zero_set, 1)
            tasks(0, 0)
            tasks(1, 1)
            with pool.Fori(1, STEPS // 2) as h:
                tasks(2 * h, 0)
                tasks(2 * h + 1, 1)
            gate(STEPS - 1, 1)

        @block.tensor
        def _(pe):
            def proj(i, b, m):
                if m == 0:
                    pe.wait_ge(hm_in[b], 16 * (i // 2 + 1))
                pe.wait_ge(w_split[m], i // NC_ + 1)
                if m == 3:
                    pe.wait_ge(conv_out, CONV * i + 1)
                elif in_loop(i, 1):
                    if m == 0:
                        pe.wait_ge(conv_out, CONV * i)
                    else:
                        pe.wait_ge(z_out, 2 * i + m - 2)
                n = 0
                for wp, hp in ((w_hi, 0), (w_hi, 1), (w_lo, 0)):
                    for kk in range(KK):
                        mm = nc.tensor.matmul(pj[m % 3][:, 0:CHUNK], wp[m][:, kk, :], hm[b][:, hp, kk, :],
                                              start=n == 0, stop=n == 3 * KK - 1)
                        n += 1
                mm.then_inc(proj_done, 1)

            def proj_z(i, b, a):
                pe.wait_ge(w_split[CONV], i // NC_ + 1)
                pe.wait_ge(conv_out, CONV * i + 2 + a)
                n = 0
                for wp, hp in ((w_hi, 0), (w_lo, 0), (w_hi, 1)):
                    for kk in range(KK):
                        mm = nc.tensor.matmul(pj[1 + a][:, 0:GW], hm[b][:, hp, kk, a * P:(a + 1) * P],
                                              wp[CONV][:, kk, :], start=n == 0, stop=n == 3 * KK - 1)
                        n += 1
                mm.then_inc(proj_done, 1)

            def step(i, b):
                j, jb = i - 1, 1 - b
                if in_loop(i):
                    for m in range(CONV):
                        proj(i, b, m)
                if in_loop(j):
                    pe.wait_ge(silu_done, j + 1)
                    if in_loop(j, 2):
                        pe.wait_ge(yt_out, j - 1)
                    for m in range(2):
                        for a in range(2):
                            tr = nc.tensor.transpose(tx[:, a * GW + m * P:a * GW + (m + 1) * P],
                                                     xbc[jb][:, m, a * P:(a + 1) * P], k.ident[:])
                    tr.then_inc(xs_tr, 1)
                    pe.wait_ge(st_done, j + 1)
                    for a in range(2):
                        tr = nc.tensor.transpose(sbp[:, a * P:(a + 1) * P], xbc[jb][:, 2, a * P:(a + 1) * P], k.ident[:])
                    tr.then_inc(b_tr, 1)
                    if in_loop(j, 1):
                        pe.wait_ge(gm_done, j)
                    nc.tensor.matmul(gp[:, 0:CHUNK], xbc[jb][:, 2, 0:P], xbc[jb][:, 3, :], start=True, stop=True)
                    nc.tensor.matmul(gp[:, CHUNK:3 * P], xbc[jb][:, 2, P:CHUNK], xbc[jb][:, 3, P:CHUNK],
                                     start=True, stop=True).then_inc(g_done, 1)
                if in_loop(i):
                    for a in range(2):
                        proj_z(i, b, a)
                if in_loop(j):
                    pe.wait_ge(w_done, 2 * (j + 1))
                    pe.wait_ge(x_done, 4 * j + 1)
                    if in_loop(j, 1):
                        pe.wait_ge(y_done, j)
                    for r in range(RH):
                        q = slice(r * HD, (r + 1) * HD)
                        nc.tensor.matmul(yi[:, r * HD:(r + 1) * HD], wt0[:, r, 0:P], xdt[:, 0, q],
                                         start=True, stop=True)
                    for r in range(RH):
                        q = slice(r * HD, (r + 1) * HD)
                        nc.tensor.matmul(yi[:, GW + r * HD:GW + (r + 1) * HD], wt0[:, r, P:CHUNK], xdt[:, 0, q],
                                         start=True, stop=False)
                        nc.tensor.matmul(yi[:, GW + r * HD:GW + (r + 1) * HD], wt1[:, r, :], xdt[:, 1, q],
                                         start=False, stop=True)
                    pe.wait_ge(st_done, j + 1)
                    for a in range(2):
                        mm = nc.tensor.matmul(yx[:, a * GW:(a + 1) * GW], xbc[jb][:, 3, a * P:(a + 1) * P], st[:],
                                              start=True, stop=True)
                    mm.then_inc(y_mm, 1)
                    pe.wait_ge(x_done, 4 * (j + 1))
                    pe.wait_ge(b_out, j + 1)
                    for a in range(2):
                        mm = nc.tensor.matmul(sbp[:, GW:2 * GW], bs[:, a, :], xend[:, a, :],
                                              start=a == 0, stop=a == 1)
                    mm.then_inc(st_mm, 1)
                if in_loop(i - 2):
                    pe.wait_ge(yn_done, 2 * (i - 1))
                    if in_loop(j):
                        pe.wait_ge(xs_out, j + 1)
                    for a in range(2):
                        for m in range(2):
                            tr = nc.tensor.transpose(tx[:, (2 * a + m) * P:(2 * a + m + 1) * P],
                                                     yn[:, a, m * P:(m + 1) * P], k.ident[:])
                    tr.then_inc(yt_tr, 1)

            step(0, 0)
            step(1, 1)
            with pe.Fori(1, STEPS // 2) as h:
                step(2 * h, 0)
                step(2 * h + 1, 1)
            step(STEPS, 0)
            step(STEPS + 1, 1)

        @block.scalar
        def _(act):
            def high(m, n):
                act.wait_ge(w_in_s[m], 16 * (n + 1))
                nc.scalar.copy(w_hi[m][:], w_raw[m][:]).then_inc(w_hi_s, 1)

            def out_conv(i, b, m):
                act.wait_ge(proj_done, 6 * i + m + 1)
                if m == 0:
                    act.wait_ge(par_ready, 2 * i + 1)
                    if in_loop(i, 2):
                        act.wait_ge(silu_done, i - 1)
                    if in_loop(i, 1):
                        act.wait_ge(halo_done, i)
                nc.scalar.copy(ub[b][:, m, TAPS - 1:], pj[m % 3][:, 0:CHUNK]).then_inc(ub_out, 1)
                nc.scalar.activation(cv[b][:, m, :], pj[m % 3][:, 0:CHUNK], ACT.Identity,
                                     bias=parb[b][:, m, TAPS:TAPS + 1], scale=parb[b][:, m, TAPS - 1:TAPS]
                                     ).then_inc(conv_out, 1)

            def exps(j, jb):
                act.wait_ge(seg_done, 8 * j + 8)
                nc.scalar.activation(seg0[:], seg0[:], ACT.Exp).then_inc(exp_done, 1)
                nc.scalar.activation(seg1[:], seg1[:], ACT.Exp).then_inc(exp_done, 1)
                if in_loop(j, 1):
                    act.wait_ge(ek_done, j)
                nc.scalar.activation(el[:], acb[jb][:, 1, :, P - 1], ACT.Exp).then_inc(el_done, 1)

            def step(i, b, first=False, last=False):
                j, jb = i - 1, 1 - b
                if in_loop(i):
                    out_conv(i, b, 0)
                    if last:
                        high(0, i // NC_ + 1)
                    if first:
                        high(CONV, i // NC_)
                if in_loop(i - 2):
                    act.wait_ge(gt_done, i - 1)
                    if in_loop(i - 3):
                        act.wait_ge(ms_done, i - 2)
                    for a in range(2):
                        nc.scalar.activation(sq[:, a], gt[:, a], ACT.Square, scale=0.5 * GW ** -0.5,
                                             accum_out=ss[:, a:a + 1]).then_inc(sq_done, 1)
                if in_loop(j):
                    exps(j, jb)
                if in_loop(i):
                    for m in range(1, CONV):
                        out_conv(i, b, m)
                        if last:
                            high(m, i // NC_ + 1)
                if in_loop(j):
                    act.wait_ge(xs_tr, j + 1)
                    if in_loop(j, 1):
                        act.wait_ge(x_done, 4 * j)
                    nc.scalar.copy(xs[:].rearrange("p a n -> p (a n)"), tx[:]).then_inc(xs_out, 1)
                    act.wait_ge(b_tr, j + 1)
                    if in_loop(j, 1):
                        act.wait_ge(st_mm, j)
                    nc.scalar.copy(bs[:].rearrange("p a n -> p (a n)"), sbp[:, 0:GW]).then_inc(b_out, 1)
                if in_loop(i):
                    for a in range(2):
                        act.wait_ge(proj_done, 6 * i + CONV + a + 1)
                        if in_loop(i, 1):
                            act.wait_ge(z_out, 2 * i + a - 1)
                        nc.scalar.activation(zth[:, a], pj[1 + a][:, 0:GW], ACT.Tanh, scale=0.5
                                             ).then_inc(zth_done, 1)
                    act.wait_ge(conv_tap, 12 * (i + 1))
                    if in_loop(i, 1):
                        act.wait_ge(silu_done, i)
                    nc.scalar.activation(th[:], cv[b][:], ACT.Tanh).then_inc(th_done, 1)
                if in_loop(i - 2):
                    act.wait_ge(yt_tr, i - 1)
                    if in_loop(i - 4):
                        act.wait_ge(y_stored[b], 32 * ((i - 4) // 2 + 1))
                    nc.scalar.copy(yt[b][:].rearrange("p a m t -> p (a m t)"), tx[:]).then_inc(yt_out, 1)
                    act.wait_ge(yt_out, i - 1)
                    c, g = (i - 2) % NC_, (i - 2) // NC_
                    for a in range(2):
                        act.dma_start(k.ytd[bass.ds(2 * c + a, 1), :, bass.ds(2 * g, 2), :]
                                      .rearrange("a p m t -> (a p) m t"), yt[b][:, a]).then_inc(y_stored[b], 16)

            for m in range(PARTS):
                high(m, 0)
            by_group(act, step)
            for b in range(2):
                act.wait_ge(y_stored[b], 16 * STEPS)

        @block.vector
        def _(dve):
            def params(i, b):
                nc.vector.tensor_copy(parb[b][:].rearrange("p m t -> p (m t)"),
                                      k.par[:, bass.ds((i // NC_), 1), :].rearrange("p g n -> p (g n)")
                                      ).then_inc(par_ready, 1)
                nc.vector.tensor_copy(tb[b][:].rearrange("p s a r -> p s (a r)"),
                                      k.tab[:, :, bass.ds(i * 2 * RH, 2 * RH)]).then_inc(par_ready, 1)

            def conv(i, b):
                if isinstance(i, int) and i == 0:
                    nc.vector.memset(ub[b][:, :, 0:TAPS - 1], 0.0).then_inc(halo_done, 1)
                else:
                    dve.wait_ge(ub_out, CONV * i)
                    nc.vector.tensor_scalar(ub[b][:, :, 0:TAPS - 1], ub[1 - b][:, :, CHUNK:CHUNK + TAPS - 1],
                                            k.keep[:, bass.ds(i, 1)], None, ALU.mult).then_inc(halo_done, 1)
                dve.wait_ge(halo_done, i + 1)
                dve.wait_ge(conv_out, CONV * (i + 1))
                for tap in range(TAPS - 1):
                    for m in range(CONV):
                        if tap:
                            dve.wait_ge(conv_tap, 12 * i + CONV * (tap - 1) + m + 1)
                        nc.vector.scalar_tensor_tensor(out=cv[b][:, m, :], in0=ub[b][:, m, tap:tap + CHUNK],
                                                       scalar=parb[b][:, m, tap:tap + 1], in1=cv[b][:, m, :],
                                                       op0=ALU.mult, op1=ALU.add).then_inc(conv_tap, 1)
                for a in range(2):
                    dve.wait_ge(zth_done, 2 * i + a + 1)
                    if in_loop(i, 2) and a == 0:
                        dve.wait_ge(gt_done, i - 1)
                    nc.vector.scalar_tensor_tensor(out=zs[b][:, a], in0=zth[:, a], scalar=1.0,
                                                   in1=pj[1 + a][:, 0:GW], op0=ALU.add, op1=ALU.mult
                                                   ).then_inc(z_out, 1)
                dve.wait_ge(th_done, i + 1)
                if in_loop(i, 2):
                    dve.wait_ge(st_mm, i - 1)
                nc.vector.scalar_tensor_tensor(out=xbc[b][:], in0=th[:], scalar=1.0, in1=cv[b][:], op0=ALU.add,
                                               op1=ALU.mult).then_inc(silu_done, 1)

            def segments(j, b):
                dve.wait_ge(ac_in[b], 16 * (j // 2 + 1))
                dve.wait_ge(par_ready, 2 * (j + 1))
                if in_loop(j, 1):
                    dve.wait_ge(w_done, 2 * j)
                    dve.wait_ge(te_done, 2 * j)
                for r in range(RH):
                    nc.vector.tensor_scalar(seg0[:, r, :].rearrange("p (a t) -> p a t", a=2), acb[b][:, :, r, :],
                                            tb[b][:, 1, 0, r:r + 1], 0.0, ALU.subtract, ALU.min
                                            ).then_inc(seg_done, 1)
                for r in range(RH):
                    nc.vector.tensor_scalar(seg1[:, r, :], acb[b][:, 1, r, :], tb[b][:, 1, 1, r:r + 1], 0.0,
                                            ALU.subtract, ALU.min).then_inc(seg_done, 1)

            def state(j):
                dve.wait_ge(el_done, j + 1)
                nc.vector.tensor_scalar(ek[:], el[:], k.keep[:, bass.ds(j + 1, 1)], None, ALU.mult
                                        ).then_inc(ek_done, 1)
                dve.wait_ge(ek_done, j + 1)
                dve.wait_ge(st_mm, j + 1)
                nc.vector.tensor_tensor(stt[:].rearrange("p (r q) -> p r q", r=RH),
                                        st[:].rearrange("p (r q) -> p r q", r=RH),
                                        ek[:].unsqueeze(2).to_broadcast([P, RH, HD]), ALU.mult
                                        ).then_inc(stt_done, 1)
                dve.wait_ge(stt_done, j + 1)
                nc.vector.scalar_tensor_tensor(out=st[:], in0=sbp[:, GW:2 * GW], scalar=k.keep[:, bass.ds(j + 1, 1)],
                                               in1=stt[:], op0=ALU.mult, op1=ALU.add).then_inc(st_done, 1)

            def combine(j, b):
                dve.wait_ge(y_mm, j + 1)
                nc.vector.tensor_tensor(t1[:].rearrange("p a (r q) -> p (a r) q", r=RH),
                                        yx[:].rearrange("p (n q) -> p n q", q=HD),
                                        tb[b][:, 2].rearrange("p a r -> p (a r)").unsqueeze(2)
                                        .to_broadcast([P, 2 * RH, HD]), ALU.mult).then_inc(t1_done, 1)
                dve.wait_ge(t1_done, j + 1)
                if in_loop(j, 1):
                    dve.wait_ge(y3_done, j)
                nc.vector.tensor_tensor(y[:].rearrange("p a n -> p (a n)"), t1[:].rearrange("p a n -> p (a n)"),
                                        yi[:], ALU.add).then_inc(y_done, 1)

            def weigh(j, b):
                dve.wait_ge(g_done, j + 1)
                nc.vector.tensor_tensor(gm[:], gp[:, 0:3 * P], k.mask3[:], ALU.mult).then_inc(gm_done, 1)
                dve.wait_ge(exp_done, 2 * (j + 1))
                if in_loop(j, 1):
                    dve.wait_ge(x_done, 4 * j)
                nc.vector.tensor_tensor(te[:, 0], seg0[:, :, CHUNK - 1], tb[b][:, 0, 0], ALU.mult).then_inc(te_done, 1)
                nc.vector.tensor_tensor(te[:, 1], seg1[:, :, P - 1], tb[b][:, 0, 1], ALU.mult).then_inc(te_done, 1)
                dve.wait_ge(gm_done, j + 1)
                if in_loop(j, 1):
                    dve.wait_ge(y_mm, j)
                nc.vector.tensor_tensor(wt0[:], seg0[:], gm[:, 0:CHUNK].unsqueeze(1).to_broadcast([P, RH, CHUNK]),
                                        ALU.mult).then_inc(w_done, 1)
                nc.vector.tensor_tensor(wt1[:], seg1[:], gm[:, CHUNK:3 * P].unsqueeze(1).to_broadcast([P, RH, P]),
                                        ALU.mult).then_inc(w_done, 1)

            def low(m, n):
                dve.wait_ge(w_hi_s, PARTS * n + m + 1)
                nc.vector.tensor_tensor(w_lo[m][:], w_raw[m][:], w_hi[m][:].bitcast(F32), ALU.subtract
                                        ).then_inc(w_split[m], 1)

            def step(i, b, first=False, last=False):
                j, jb = i - 1, 1 - b
                if in_loop(i - 2):
                    combine(i - 2, b)
                    state(i - 2)
                if in_loop(i):
                    if in_loop(i, 2):
                        dve.wait_ge(x_done, 4 * (i - 1))
                        dve.wait_ge(t1_done, i - 1)
                    params(i, b)
                if in_loop(j):
                    segments(j, jb)
                if first:
                    low(CONV, i // NC_)
                if in_loop(i - 2):
                    dve.wait_ge(rs_done, i - 1)
                    dve.wait_ge(gw_done, 2 * (i - 1))
                    if in_loop(i - 3):
                        dve.wait_ge(yt_tr, i - 2)
                    for a in range(2):
                        nc.vector.tensor_scalar(yn[:, a], gw[:, a], rs[:, a:a + 1], None, ALU.mult
                                                ).then_inc(yn_done, 1)
                if last:
                    low(0, i // NC_ + 1)
                if in_loop(j):
                    weigh(j, jb)
                if last:
                    for m in range(1, CONV):
                        low(m, i // NC_ + 1)
                if in_loop(i):
                    conv(i, b)

            nc.vector.memset(st[:], 0.0).then_inc(st_done, 1)
            for m in range(PARTS):
                low(m, 0)
            by_group(dve, step)


def row_vectors(nc, k, w_hi, w_lo):
    with ExitStack() as ctx:
        sb, ps, sem = k.makers(ctx)
        NW = 3
        wa = [sb(f"wr{b}", [P, KK, 512]) for b in range(2)]
        wraw = [sb(f"wo_raw{b}", [P, D]) for b in range(NW)]
        csb = sb("csb", [P, KK, P])
        lng, lnb = sb("lng", [P, D]), sb("lnb", [P, D])
        rp = [ps(f"rp{b}", [P, 512]) for b in range(2)]
        rows = [k.g1, k.b2, k.a2, k.g2]
        bias_in, cs_wide, row_mm, row_out, chain = (sem(n) for n in "bias_in cs_wide row_mm row_full chain_r".split())
        wr_in = [sem(f"wr_in{b}") for b in range(2)]
        wo_in = [sem(f"wo_in{b}") for b in range(NW)]
        hi_done, lo_done = sem("wo_hi_done"), sem("wo_lo_done")
        block = ctx.enter_context(nc.Block())
        w_ada = k.d["w_ada"].rearrange("(kk p) n -> p kk n", p=P)

        @block.sync
        def _(sp):
            for n, row in enumerate(rows):
                sp.dma_start(row[:], k.d["b_ada"][0, (2 + n) * D:(3 + n) * D].partition_broadcast(P)
                             ).then_inc(bias_in, 16)
            sp.dma_start(lng[:], k.d["ln_g"][0].partition_broadcast(P)).then_inc(bias_in, 16)
            sp.dma_start(lnb[:], k.d["ln_b"][0].partition_broadcast(P)).then_inc(bias_in, 16)
            for s in range(8):
                if s >= 2:
                    sp.wait_ge(row_mm, s - 1)
                sp.dma_start(wa[s % 2][:], w_ada[:, :, 2 * D + s * 512:2 * D + (s + 1) * 512]
                             ).then_inc(wr_in[s % 2], 16)

        @block.scalar
        def _(act):
            for m in range(NW):
                act.dma_start(wraw[m][:], k.d["w_out"][m * P:(m + 1) * P, :]).then_inc(wo_in[m], 16)
            for m in range(YTILES):
                act.wait_ge(wo_in[m % NW], 16 * (m // NW + 1))
                nc.scalar.copy(w_hi[:, m, :], wraw[m % NW][:]).then_inc(hi_done, 1)
                n = m - 1 + NW
                if m >= 1 and n < YTILES:
                    act.wait_ge(lo_done, m)
                    act.dma_start(wraw[n % NW][:], k.d["w_out"][n * P:(n + 1) * P, :]).then_inc(wo_in[n % NW], 16)

        @block.tensor
        def _(pe):
            pe.wait_ge(cs_wide, KK)
            for s in range(8):
                pe.wait_ge(wr_in[s % 2], 16 * (s // 2 + 1))
                if s >= 2:
                    pe.wait_ge(row_out, s - 1)
                for kk in range(KK):
                    mm = nc.tensor.matmul(rp[s % 2][:], csb[:, kk, :], wa[s % 2][:, kk, :],
                                          start=kk == 0, stop=kk == KK - 1)
                mm.then_inc(row_mm, 1)

        @block.vector
        def _(dve):
            for kk in range(KK):
                nc.vector.tensor_scalar(csb[:, kk, :], k.ones[:], k.cs[:, kk:kk + 1], None, ALU.mult
                                        ).then_inc(cs_wide, 1)

            def low(m):
                dve.wait_ge(hi_done, m + 1)
                nc.vector.tensor_tensor(w_lo[:, m, :], wraw[m % NW][:], w_hi[:, m, :].bitcast(F32), ALU.subtract
                                        ).then_inc(lo_done, 1)

            dve.wait_ge(bias_in, 16 * 6)
            for s in range(8):
                low(2 * s)
                low(2 * s + 1)
                dve.wait_ge(row_mm, s + 1)
                half = rows[s // 2][:, (s % 2) * 512:(s % 2 + 1) * 512]
                nc.vector.scalar_tensor_tensor(out=half, in0=rp[s % 2][:], scalar=0.0 if s // 2 == 1 else 1.0,
                                               in1=half, op0=ALU.add, op1=ALU.add).then_inc(row_out, 1)
            dve.wait_ge(row_out, 8)
            nc.vector.tensor_tensor(lnb[:], k.a2[:], lnb[:], ALU.mult).then_inc(chain, 1)
            dve.wait_ge(chain, 1)
            nc.vector.tensor_tensor(k.b2[:], k.b2[:], lnb[:], ALU.add).then_inc(chain, 1)
            nc.vector.tensor_tensor(k.a2[:], k.a2[:], lng[:], ALU.mult).then_inc(chain, 1)
            dve.wait_ge(chain, 3)


def out_projection(nc, k, w_hi, w_lo, lgP):
    with ExitStack() as ctx:
        sb, ps, sem = k.makers(ctx)
        yraw = sb("yraw", [P, YTILES, P])
        yhi = [sb(f"yhi{b}", [P, YTILES, P], F32R) for b in range(2)]
        ylo = [sb(f"ylo{b}", [P, YTILES, P], F32R) for b in range(2)]
        xt = [sb("xo", [P, D])] * 2
        r, h2, h2t = sb("r", [P, D]), sb("h2", [P, D]), sb("h2t", [P, KK, P])
        wr = sb("w_router", [P, KK, EXPERTS])
        bst, mv, ve, nmr = sb("bst", [P, 2, 6]), sb("mv", [P, 2]), sb("ve", [P, 1]), sb("nmr", [P, 1])
        rstd = sb("rstd", [P, 1])
        op = [[ps(f"op{b}{n}", [P, 512]) for n in range(2)] for b in range(2)]
        tp = [ps(f"tp{n}", [P, 512]) for n in range(2)]
        (y_in, wr_in, hi_done, lo_done, o_mm, t_done, r_done, bn_done, mv_done, ve_done, rstd_done, nmr_done,
         xn_done, xn_out, ha_done, h2_done, h2_out, tr_done, ht_done, lg_mm) = (sem(n) for n in (
             "y_in wr_in yhi_done ylo_done o_mm t_done r_done bn_done mv_done ve_done rstd_done nmr_done "
             "xn_done xn_out ha_done h2_done h2_out trh_done ht_done lg_mm").split())
        x_in = [sem(f"xo_in{b}") for b in range(2)]
        block = ctx.enter_context(nc.Block())

        def loop(eng, step, extra=0):
            step(0, 0)
            step(1, 1)
            with eng.Fori(1, TT // 2) as h:
                step(2 * h, 0)
                step(2 * h + 1, 1)
            for i in range(extra):
                step(TT + i, i % 2)

        @block.sync
        def _(sp):
            sp.dma_start(wr[:], k.d["w_router"].rearrange("(kk p) e -> p kk e", p=P)).then_inc(wr_in, 16)

            def step(i, b):
                if in_loop(i, 1):
                    sp.wait_ge(lo_done, i)
                sp.dma_start(yraw[:], k.ytd[bass.ds(i, 1)].rearrange("a p m t -> (a p) m t")).then_inc(y_in, 16)
                if in_loop(i, 1):
                    sp.wait_ge(r_done, i)
                sp.dma_start(xt[b][:], k.d["x"].rearrange("(a p) n -> a p n", p=P)[bass.ds(i, 1)]
                             .rearrange("a p n -> (a p) n")).then_inc(x_in[b], 16)

            loop(sp, step)

        @block.gpsimd
        def _(pool):
            def step(i, b):
                if i is not None:
                    pool.wait_ge(ve_done, i + 1)
                if in_loop(i, 1):
                    pool.wait_ge(xn_done, i)
                nc.gpsimd.tensor_tensor(rstd[:], ve[:], k.negh[:, 0:1], ALU.pow).then_inc(rstd_done, 1)

            loop(pool, step)

        @block.tensor
        def _(pe):
            def step(i, b):
                if in_loop(i, 0, TT):
                    pe.wait_ge(lo_done, i + 1)
                    if in_loop(i, 2, TT):
                        pe.wait_ge(t_done, 2 * (i - 1))
                    for n in range(2):
                        q = 0
                        for yp, wp in ((yhi, w_hi), (yhi, w_lo), (ylo, w_hi)):
                            for m in range(YTILES):
                                mm = nc.tensor.matmul(op[b][n][:], yp[b][:, m, :], wp[:, m, n * 512:(n + 1) * 512],
                                                      start=q == 0, stop=q == 3 * YTILES - 1)
                                q += 1
                        mm.then_inc(o_mm, 1)
                if in_loop(i, 1, TT + 1):
                    j = i - 1
                    pe.wait_ge(h2_done, j + 1)
                    if in_loop(j, 1):
                        pe.wait_ge(ht_done, 2 * j)
                    for n in range(2):
                        for q in range(4):
                            tr = nc.tensor.transpose(tp[n][:, q * P:(q + 1) * P],
                                                     h2[:, (4 * n + q) * P:(4 * n + q + 1) * P], k.ident[:])
                        tr.then_inc(tr_done, 1)
                    pe.wait_ge(ht_done, 2 * (j + 1))
                    if not in_loop(j, 1):
                        pe.wait_ge(wr_in, 16)
                    for kk in range(KK):
                        mm = nc.tensor.matmul(lgP[:, bass.ds(j * EXPERTS, EXPERTS)], h2t[:, kk, :], wr[:, kk, :],
                                              start=kk == 0, stop=kk == KK - 1)
                    mm.then_inc(lg_mm, 1)

            loop(pe, step, 1)

        @block.scalar
        def _(act):
            def split(i, b):
                act.wait_ge(y_in, 16 * (i + 1))
                if in_loop(i, 2):
                    act.wait_ge(o_mm, 2 * (i - 1))
                nc.scalar.copy(yhi[b][:], yraw[:]).then_inc(hi_done, 1)

            def step(i, b):
                if in_loop(i, 0, TT):
                    split(i, b)
                j = i - 1
                if in_loop(j, 0, TT):
                    act.wait_ge(nmr_done, j + 1)
                    nc.scalar.activation(r[:], r[:], ACT.Identity, bias=nmr[:], scale=rstd[:]).then_inc(xn_done, 1)
                    act.wait_ge(xn_done, j + 1)
                    act.dma_start(k.xnd[bass.ds(j, 1)].rearrange("a p n -> (a p) n"), r[:]).then_inc(xn_out, 16)
                    act.wait_ge(h2_done, j + 1)
                    if in_loop(j, 1, TT):
                        act.wait_ge(h2_out, 16 * j)
                    act.dma_start(k.h2d[bass.ds(j * P, P), :], h2[:]).then_inc(h2_out, 16)
                    if in_loop(j, 1, TT):
                        act.wait_ge(lg_mm, j)
                    for n in range(2):
                        act.wait_ge(tr_done, 2 * j + n + 1)
                        nc.scalar.copy(h2t[:, 4 * n:4 * n + 4, :].rearrange("p q t -> p (q t)"), tp[n][:]
                                       ).then_inc(ht_done, 1)

            loop(act, step, 1)
            act.wait_ge(xn_out, 16 * TT)
            act.wait_ge(h2_out, 16 * TT)

        @block.vector
        def _(dve):
            def low(i, b):
                dve.wait_ge(hi_done, i + 1)
                if in_loop(i, 2):
                    dve.wait_ge(o_mm, 2 * (i - 1))
                nc.vector.tensor_tensor(ylo[b][:], yraw[:], yhi[b][:].bitcast(F32), ALU.subtract
                                        ).then_inc(lo_done, 1)

            def step(i, b):
                if in_loop(i, 0, TT):
                    low(i, b)
                j, jb = i - 1, 1 - b
                if not in_loop(j, 0, TT):
                    return
                if in_loop(j, 1):
                    dve.wait_ge(xn_out, 16 * j)
                    dve.wait_ge(ha_done, j)
                for n in range(2):
                    dve.wait_ge(o_mm, 2 * j + n + 1)
                    nc.vector.tensor_tensor(r[:, n * 512:(n + 1) * 512], op[jb][n][:],
                                            k.g1[:, n * 512:(n + 1) * 512], ALU.mult).then_inc(t_done, 1)
                dve.wait_ge(x_in[jb], 16 * (j // 2 + 1))
                dve.wait_ge(t_done, 2 * (j + 1))
                nc.vector.scalar_tensor_tensor(out=r[:], in0=xt[jb][:], scalar=ALPHA, in1=r[:], op0=ALU.mult,
                                               op1=ALU.add).then_inc(r_done, 1)
                dve.wait_ge(r_done, j + 1)
                for n in range(2):
                    nc.vector.bn_stats(bst[:, n, :], r[:, n * 512:(n + 1) * 512]).then_inc(bn_done, 1)
                dve.wait_ge(bn_done, 2 * (j + 1))
                dve.sem_inc(k.passed, 1)
                nc.vector.bn_aggr(mv[:], bst[:].rearrange("p a b -> p (a b)")).then_inc(mv_done, 1)
                dve.wait_ge(mv_done, j + 1)
                nc.vector.tensor_scalar(ve[:], mv[:, 1:2], EPS, None, ALU.add).then_inc(ve_done, 1)
                dve.wait_ge(rstd_done, j + 1)
                nc.vector.scalar_tensor_tensor(out=nmr[:], in0=mv[:, 0:1], scalar=-1.0, in1=rstd[:], op0=ALU.mult,
                                               op1=ALU.mult).then_inc(nmr_done, 1)
                dve.wait_ge(xn_done, j + 1)
                if in_loop(j, 1):
                    dve.wait_ge(tr_done, 2 * j)
                    dve.wait_ge(h2_out, 16 * j)
                nc.vector.tensor_tensor(h2[:], r[:], k.a2[:], ALU.mult).then_inc(ha_done, 1)
                dve.wait_ge(ha_done, j + 1)
                nc.vector.tensor_tensor(h2[:], h2[:], k.b2[:], ALU.add).then_inc(h2_done, 1)

            loop(dve, step, 1)


def route(nc, k, lgP):
    with ExitStack() as ctx:
        sb, ps, sem = k.makers(ctx)
        E, N = EXPERTS, TT * EXPERTS
        G4 = TT * EGROUPS
        rb = sb("rb", [P, E])
        p, eq, oh1, oh2, pm, cand = (sb(n, [P, N]) for n in "p eq oh1 oh2 pm cand".split())
        mx, sm = sb("mx", [P, TT]), sb("sm", [P, TT])
        m1, m2, i1, gs, gh = (sb(n, [P, G4]) for n in "m1 m2 i1 gs gh".split())
        off, cnt, base = sb("off", [P, TT + 1, E]), sb("cnt", [P, N]), sb("base", [P, E])
        nt, end = sb("nt", [P, E]), sb("end", [P, E])
        cmp = sb("cmp", [P, MAXT, E])
        ef, pf = sb("ef", [P, MAXT]), sb("pf", [P, 1])
        slf = sb("slf", [P, TT])
        zero = sb("zero", [MAXT + 1, P])
        idr = sb("idr", [MAXT + 1, P])
        pre, cnp, idp = ps("pre", [P, 512]), ps("cnp", [P, 512]), ps("idp", [P, 512])
        chain, rb_in, exp_done, cnt_mm, zero_out, zset, scat, id_in, id_tr, slot_ready = (sem(n) for n in (
            "chain_q rb_in exp_q cnt_mm zslot_out zset scat id_in id_tr slot_ready").split())
        block = ctx.enter_context(nc.Block())

        @block.sync
        def _(sp):
            sp.dma_start(rb[:], k.d["b_router"].partition_broadcast(P)).then_inc(rb_in, 16)
            sp.wait_ge(zset, 1)
            sp.dma_start(k.slotd.rearrange("(a b) c -> a (b c)", b=P), zero[:]).then_inc(zero_out, 16)
            sp.wait_ge(scat, 16 * 2 * TT)
            sp.dma_start(idr[:], k.slotd.rearrange("(a b) c -> a (b c)", b=P)).then_inc(id_in, 16)

        @block.gpsimd
        def _(pool):
            nc.gpsimd.memset(zero[:], 0.0).then_inc(zset, 1)
            pool.wait_ge(zero_out, 16)
            pool.wait_ge(slot_ready, 2)
            for t in range(TT):
                for slots in (k.slot_a, k.slot_b):
                    nc.gpsimd.indirect_dma_start(
                        out=k.slotd[:], out_offset=bass.IndirectOffsetOnAxis(ap=slots[:, t:t + 1], axis=0),
                        in_=k.tok[:, t:t + 1], in_offset=None).then_inc(scat, 16)
            pool.wait_ge(scat, 16 * 2 * TT)

        @block.scalar
        def _(act):
            act.wait_ge(chain, 3)
            nc.scalar.activation(p[:], p[:], ACT.Exp).then_inc(exp_done, 1)

        @block.tensor
        def _(pe):
            pe.wait_ge(slot_ready, 1)
            nc.tensor.matmul(pre[:], k.below[:], eq[:], start=True, stop=True)
            nc.tensor.matmul(cnp[:], k.ones[:], eq[:], start=True, stop=True).then_inc(cnt_mm, 1)
            pe.wait_ge(id_in, 16)
            nc.tensor.transpose(idp[:, 0:MAXT + 1], idr[:], k.ident[0:MAXT + 1, 0:MAXT + 1]).then_inc(id_tr, 1)

        @block.vector
        def _(dve):
            count = [0]

            def link(ins):
                count[0] += 1
                ins.then_inc(chain, 1)
                dve.wait_ge(chain, count[0])

            v = nc.vector

            def over(ap, n, m):
                return ap.unsqueeze(2).to_broadcast([P, n, m])

            def along(ap, n, m):
                return ap.unsqueeze(1).to_broadcast([P, n, m])

            def rows(t, m):
                return t[:].rearrange("p (n m) -> p n m", m=m)

            dve.wait_ge(rb_in, 16)
            link(v.tensor_tensor(rows(p, E), lgP[:].rearrange("p (n m) -> p n m", m=E), along(rb[:], TT, E), ALU.add))
            link(v.tensor_reduce(mx[:], rows(p, E), AX.X, ALU.max))
            link(v.tensor_tensor(rows(p, E), rows(p, E), over(mx[:], TT, E), ALU.subtract))
            dve.wait_ge(exp_done, 1)
            link(v.tensor_reduce(sm[:], rows(p, E), AX.X, ALU.add))
            link(v.reciprocal(sm[:], sm[:]))
            link(v.tensor_tensor(rows(p, E), rows(p, E), over(sm[:], TT, E), ALU.mult))

            def first_max(values, m, n, w, idx, hot):
                link(v.tensor_reduce(m, values, AX.X, ALU.max))
                link(v.tensor_tensor(hot, values, over(m, n, w), ALU.is_equal))
                link(v.scalar_tensor_tensor(out=cand[:, 0:n * w].rearrange("p (n m) -> p n m", m=w), in0=hot,
                                            scalar=-float(EPG), in1=along(k.eidx[:, 0:w], n, w), op0=ALU.mult,
                                            op1=ALU.add))
                link(v.tensor_reduce(idx, cand[:, 0:n * w].rearrange("p (n m) -> p n m", m=w), AX.X, ALU.min))
                link(v.tensor_scalar(idx, idx, float(EPG), None, ALU.add))
                link(v.tensor_tensor(hot, along(k.eidx[:, 0:w], n, w), over(idx, n, w), ALU.is_equal))

            first_max(rows(p, EPG), m1[:], G4, EPG, i1[:], rows(oh1, EPG))
            link(v.scalar_tensor_tensor(out=pm[:], in0=oh1[:], scalar=-4.0, in1=p[:], op0=ALU.mult, op1=ALU.add))
            first_max(rows(pm, EPG), m2[:], G4, EPG, i1[:], rows(oh2, EPG))
            link(v.tensor_tensor(gs[:], m1[:], m2[:], ALU.add))
            first_max(rows(gs, EGROUPS), mx[:], TT, EGROUPS, sm[:], rows(gh, EGROUPS))
            for oh in (oh1, oh2):
                link(v.tensor_tensor(rows(oh, EPG), rows(oh, EPG), over(gh[:], G4, EPG), ALU.mult))
            for m, g in ((m1, k.gate_a), (m2, k.gate_b)):
                link(v.tensor_tensor(m[:], m[:], gh[:], ALU.mult))
                link(v.tensor_reduce(g[:], rows(m, EGROUPS), AX.X, ALU.add))
            link(v.tensor_tensor(sm[:], k.gate_a[:], k.gate_b[:], ALU.add))
            link(v.reciprocal(sm[:], sm[:]))
            for g in (k.gate_a, k.gate_b):
                link(v.tensor_tensor(g[:], g[:], sm[:], ALU.mult))
            v.tensor_tensor(eq[:], oh1[:], oh2[:], ALU.add).then_inc(slot_ready, 1)
            dve.wait_ge(cnt_mm, 1)
            link(v.tensor_copy(cnt[:], cnp[:]))
            link(v.memset(off[:, 0, :], 0.0))
            for t in range(TT):
                link(v.tensor_tensor(off[:, t + 1, :], off[:, t, :], cnt[:, t * E:(t + 1) * E], ALU.add))
            link(v.tensor_scalar(ef[:], k.tidx[:], float(P), None, ALU.mult))
            link(v.tensor_tensor(cmp[:, 0:TT, :].rearrange("p a b -> p (a b)").rearrange("p (e j) -> p e j", j=TT),
                                 over(off[:, TT, :], E, TT), along(ef[:, 0:TT], E, TT), ALU.is_gt))
            link(v.tensor_reduce(nt[:], cmp[:, 0:TT, :].rearrange("p a b -> p (a b)").rearrange("p (e j) -> p e j", j=TT),
                                 AX.X, ALU.add))
            link(v.tensor_tensor_scan(end[:], k.ones[:, 0:E], nt[:], 0.0, ALU.mult, ALU.add))
            link(v.tensor_tensor(base[:], end[:], nt[:], ALU.subtract))
            link(v.tensor_scalar(base[:], base[:], float(P), None, ALU.mult))
            link(v.tensor_tensor(cand[:], pre[:], off[:, 0:TT, :].rearrange("p a b -> p (a b)"), ALU.add))
            link(v.tensor_tensor(rows(cand, E), rows(cand, E), along(base[:], TT, E), ALU.add))
            for oh, slots in ((oh1, k.slot_a), (oh2, k.slot_b)):
                link(v.tensor_tensor(pm[:], cand[:], oh[:], ALU.mult))
                link(v.tensor_reduce(slf[:], rows(pm, E), AX.X, ALU.add))
                link(v.tensor_copy(slots[:], slf[:]))
            v.memset(pf[:], 0.0).then_inc(slot_ready, 1)
            link(v.tensor_tensor(cmp[:], along(end[:], MAXT, E), over(k.tidx[:], MAXT, E), ALU.is_le))
            link(v.tensor_reduce(ef[:], cmp[:], AX.X, ALU.add))
            link(v.tensor_scalar(ef[:], ef[:], float(E - 1), None, ALU.min))
            link(v.tensor_copy(k.tile_expert[:], ef[:]))
            link(v.tensor_scalar(ef[:, 0:MAXT // 2], k.tidx[:, 0:MAXT // 2], 2.0, None, ALU.mult))
            link(v.tensor_scalar(cmp[:, 0, :], ef[:, 0:MAXT // 2], end[:, E - 1:E], None, ALU.is_lt))
            link(v.tensor_reduce(sm[:, 0:1], cmp[:, 0, :], AX.X, ALU.add))
            link(v.tensor_scalar(k.last_pair[:], sm[:, 0:1], -1.0, None, ALU.add))
            dve.wait_ge(id_tr, 1)
            link(v.tensor_copy(k.ids[:], idp[:, 0:MAXT + 1]))


def experts(nc, k):
    with ExitStack() as ctx:
        sb, ps, sem = k.makers(ctx)
        wg = [sb(f"wg{b}", [P, KK, FE]) for b in range(2)]
        wu = [sb(f"wu{b}", [P, KK, FE]) for b in range(2)]
        wd = [sb(f"wd{b}", [P, FE // P, D]) for b in range(2)]
        ix = [sb(f"ix{b}", [P, 1], I32) for b in range(2)]
        xg = [sb(f"xg{b}", [P, D]) for b in range(2)]
        xt = [sb(f"xt_{b}", [P, KK, P]) for b in range(2)]
        th, a, h = sb("th_e", [P, FE]), sb("a_e", [P, FE]), sb("h_e", [P, FE])
        ht = [sb(f"ht{b}", [P, FE // P, P]) for b in range(2)]
        ye = [sb(f"ye{b}", [P, D]) for b in range(2)]
        xp = [ps(f"xp{n}", [P, 512]) for n in range(2)]
        gp, up, hp = ps("gp_e", [P, 512]), ps("up_e", [P, 512]), ps("hp_e", [P, 512])
        yp = [ps(f"yp{n}", [P, 512]) for n in range(2)]
        wgu_in = [sem(f"wgu_in{b}") for b in range(2)]
        wd_in = [sem(f"wd_in{b}") for b in range(2)]
        x_in = [sem(f"xg_in{b}") for b in range(2)]
        ye_out = [sem(f"ye_out{b}") for b in range(2)]
        (ix_ready, x_tr, xt_done, gate_mm, gu_mm, th_done, a_done, h_done, h_tr, ht_done, d_mm, ye_done) = (
            sem(n) for n in "ix_ready x_tr xt_done gate_mm gu_mm the_done a_done h_done h_tr hte_done d_mm ye_done".split())
        block = ctx.enter_context(nc.Block())

        def loop(eng, step):
            last = eng.value_load(k.last_pair[0:1, 0:1], min_val=TT - 1, max_val=MAXT // 2 - 1)
            step(0, 0)
            step(1, 1)
            with eng.Fori(1, last + 1) as q:
                step(2 * q, 0)
                step(2 * q + 1, 1)
            return last

        @block.sync
        def _(sp):
            def step(t, b):
                e = sp.value_load(k.tile_expert[0:1, bass.ds(t, 1)], min_val=0, max_val=EXPERTS - 1)
                if in_loop(t, 2):
                    sp.wait_ge(gu_mm, t - 1)
                for w, name in ((wg, "w_gate"), (wu, "w_up")):
                    sp.dma_start(w[b][:], k.d[name][bass.ds(e, 1)].rearrange("e (kk p) f -> p (e kk) f", p=P)
                                 ).then_inc(wgu_in[b], 16)
                if in_loop(t, 2):
                    sp.wait_ge(d_mm, 2 * (t - 1))
                sp.dma_start(wd[b][:], k.d["w_down"][bass.ds(e, 1)].rearrange("e (kk p) f -> p (e kk) f", p=P)
                             ).then_inc(wd_in[b], 16)

            loop(sp, step)

        @block.gpsimd
        def _(pool):
            def step(t, b):
                if in_loop(t, 2):
                    pool.wait_ge(x_tr, 2 * (t - 1))
                    pool.sem_inc(k.passed, 1)
                nc.gpsimd.tensor_copy(ix[b][:], k.ids[:, bass.ds(t, 1)]).then_inc(ix_ready, 1)
                pool.wait_ge(ix_ready, t + 1)
                pool.sem_inc(k.passed, 1)
                nc.gpsimd.indirect_dma_start(out=xg[b][:], out_offset=None, in_=k.h2d[:],
                                             in_offset=bass.IndirectOffsetOnAxis(ap=ix[b][:], axis=0)
                                             ).then_inc(x_in[b], 16)

            last = loop(pool, step)
            step(2 * last + 2, 0)
            pool.wait_ge(x_in[0], 16 * (last + 2))
            pool.sem_inc(k.passed, 1)

        @block.tensor
        def _(pe):
            def turn(t, b):
                pe.wait_ge(x_in[b], 16 * (t // 2 + 1))
                if in_loop(t, 1):
                    pe.wait_ge(xt_done, 2 * t)
                for n in range(2):
                    for q in range(4):
                        tr = nc.tensor.transpose(xp[n][:, q * P:(q + 1) * P],
                                                 xg[b][:, (4 * n + q) * P:(4 * n + q + 1) * P], k.ident[:])
                    tr.then_inc(x_tr, 1)

            def down(t, b):
                pe.wait_ge(ht_done, t + 1)
                pe.wait_ge(wd_in[b], 16 * (t // 2 + 1))
                for n in range(2):
                    if in_loop(t, 1):
                        pe.wait_ge(ye_done, 2 * t + n - 1)
                    for q in range(FE // P):
                        mm = nc.tensor.matmul(yp[n][:], ht[b][:, q, :], wd[b][:, q, n * 512:(n + 1) * 512],
                                              start=q == 0, stop=q == FE // P - 1)
                    mm.then_inc(d_mm, 1)

            def step(t, b):
                pe.wait_ge(xt_done, 2 * (t + 1))
                pe.wait_ge(wgu_in[b], 32 * (t // 2 + 1))
                if in_loop(t, 1):
                    pe.wait_ge(h_done, t)
                for w, acc in ((wg, gp), (wu, up)):
                    for kk in range(KK):
                        mm = nc.tensor.matmul(acc[:], xt[b][:, kk, :], w[b][:, kk, :], start=kk == 0, stop=kk == KK - 1)
                    mm.then_inc(gate_mm if w is wg else gu_mm, 1)
                turn(t + 1, 1 - b)
                if in_loop(t, 1):
                    down(t - 1, 1 - b)
                pe.wait_ge(h_done, t + 1)
                if in_loop(t, 1):
                    pe.wait_ge(ht_done, t)
                for q in range(FE // P):
                    tr = nc.tensor.transpose(hp[:, q * P:(q + 1) * P], h[:, q * P:(q + 1) * P], k.ident[:])
                tr.then_inc(h_tr, 1)

            turn(0, 0)
            last = loop(pe, step)
            down(2 * last + 1, 1)

        @block.scalar
        def _(act):
            def xt_copy(t, b):
                if in_loop(t, 2):
                    act.wait_ge(gu_mm, t - 1)
                for n in range(2):
                    act.wait_ge(x_tr, 2 * t + n + 1)
                    nc.scalar.copy(xt[b][:, 4 * n:4 * n + 4, :].rearrange("p q t -> p (q t)"), xp[n][:]
                                   ).then_inc(xt_done, 1)

            def ye_copy(t, b):
                if in_loop(t, 2):
                    act.wait_ge(ye_out[b], 16 * (t // 2))
                for n in range(2):
                    act.wait_ge(d_mm, 2 * t + n + 1)
                    nc.scalar.copy(ye[b][:, n * 512:(n + 1) * 512], yp[n][:]).then_inc(ye_done, 1)
                act.wait_ge(ye_done, 2 * (t + 1))
                act.dma_start(k.ysd[bass.ds(t * P, P), :], ye[b][:]).then_inc(ye_out[b], 16)

            def step(t, b):
                act.wait_ge(gate_mm, t + 1)
                if in_loop(t, 1):
                    act.wait_ge(a_done, t)
                nc.scalar.activation(th[:], gp[:], ACT.Tanh, scale=0.5).then_inc(th_done, 1)
                xt_copy(t + 1, 1 - b)
                if in_loop(t, 1):
                    ye_copy(t - 1, 1 - b)
                act.wait_ge(h_tr, t + 1)
                if in_loop(t, 2):
                    act.wait_ge(d_mm, 2 * (t - 1))
                nc.scalar.activation(ht[b][:].rearrange("p q t -> p (q t)"), hp[:], ACT.Copy, scale=0.5
                                     ).then_inc(ht_done, 1)

            xt_copy(0, 0)
            last = loop(act, step)
            ye_copy(2 * last + 1, 1)
            for b in range(2):
                act.wait_ge(ye_out[b], 16 * (last + 1))
                act.sem_inc(k.passed, 1)

        @block.vector
        def _(dve):
            def step(t, b):
                dve.wait_ge(th_done, t + 1)
                nc.vector.scalar_tensor_tensor(out=a[:], in0=th[:], scalar=1.0, in1=gp[:], op0=ALU.add,
                                               op1=ALU.mult).then_inc(a_done, 1)
                dve.wait_ge(a_done, t + 1)
                dve.wait_ge(gu_mm, t + 1)
                if in_loop(t, 1):
                    dve.wait_ge(h_tr, t)
                nc.vector.tensor_tensor(h[:], a[:], up[:], ALU.mult).then_inc(h_done, 1)

            loop(dve, step)


def output(nc, k, out):
    with ExitStack() as ctx:
        sb, ps, sem = k.makers(ctx)
        a1, b1, lng, lnb = (sb(n, [P, D]) for n in "a1 b1 lng2 lnb2".split())
        ia, ib = [sb(f"ia{b}", [P, 1], I32) for b in range(2)], [sb(f"ib{b}", [P, 1], I32) for b in range(2)]
        ga, gb = [sb(f"ga{b}", [P, 1]) for b in range(2)], [sb(f"gb{b}", [P, 1]) for b in range(2)]
        ya, yb = [sb(f"ya{b}", [P, D]) for b in range(2)], [sb(f"yb{b}", [P, D]) for b in range(2)]
        xn = [sb(f"xn{b}", [P, D]) for b in range(2)]
        m, r, o = ([sb(f"{n}{b}", [P, D]) for b in range(2)] for n in ("m_", "r_", "o_"))
        bst, mv, ve, nmr = sb("bst2", [P, 2, 6]), sb("mv2", [P, 2]), sb("ve2", [P, 1]), sb("nmr2", [P, 1])
        rstd = sb("rstd2", [P, 1])
        (row_in, row_ready, cols, xq_done, xb_done, mg_done, ms_done, mm_done, r_done, bn_done, mv_done, ve_done,
         rstd_done, nmr_done, n_done, og_done, o_done) = (sem(n) for n in (
             "row_in row_ready2 cols xq_done xb_done mg_done msum_done mm_done2 r2_done bn2 mv2s ve2s rstd2s nmr2s "
             "n_done og_done o_done").split())
        ya_in, yb_in, xn_in, stored = ([sem(f"{n}{b}") for b in range(2)] for n in ("ya_in", "yb_in", "xn_in", "stored"))
        block = ctx.enter_context(nc.Block())

        def loop(eng, step, extra=0):
            step(0, 0)
            step(1, 1)
            with eng.Fori(1, TT // 2) as q:
                step(2 * q, 0)
                step(2 * q + 1, 1)
            for i in range(extra):
                step(TT + i, i % 2)

        @block.sync
        def _(sp):
            for row, src in ((a1, k.d["ln_g"][0]), (b1, k.d["ln_b"][0]), (lng, k.d["ln_g"][1]), (lnb, k.d["ln_b"][1])):
                sp.dma_start(row[:], src.partition_broadcast(P)).then_inc(row_in, 16)

            def step(i, b):
                if in_loop(i, 2):
                    sp.wait_ge(r_done, i - 1)
                sp.dma_start(xn[b][:], k.xnd[bass.ds(i, 1)].rearrange("a p n -> (a p) n")).then_inc(xn_in[b], 16)
                if in_loop(i, 2):
                    sp.wait_ge(o_done, i - 1)
                    sp.dma_start(out[bass.ds((i - 2) * P, P), :], o[b][:]).then_inc(stored[b], 16)

            loop(sp, step)
            for i in range(TT - 2, TT):
                sp.wait_ge(o_done, i + 1)
                sp.dma_start(out[i * P:(i + 1) * P, :], o[i % 2][:]).then_inc(stored[i % 2], 16)
            for b in range(2):
                sp.wait_ge(stored[b], 16 * TT // 2)

        @block.gpsimd
        def _(pool):
            def fetch(i, b):
                if in_loop(i, 2):
                    pool.wait_ge(ms_done, i - 1)
                    pool.sem_inc(k.passed, 1)
                for dst, src in ((ia, k.slot_a), (ib, k.slot_b), (ga, k.gate_a), (gb, k.gate_b)):
                    nc.gpsimd.tensor_copy(dst[b][:], src[:, bass.ds(i, 1)]).then_inc(cols, 1)
                pool.wait_ge(cols, 4 * (i + 1))
                pool.sem_inc(k.passed, 1)
                for idx, y, s in ((ia, ya, ya_in), (ib, yb, yb_in)):
                    nc.gpsimd.indirect_dma_start(out=y[b][:], out_offset=None, in_=k.ysd[:],
                                                 in_offset=bass.IndirectOffsetOnAxis(ap=idx[b][:], axis=0)
                                                 ).then_inc(s[b], 16)

            def step(i, b):
                if in_loop(i, 0, TT):
                    fetch(i, b)
                j, jb = i - 1, 1 - b
                if in_loop(j, 0, TT):
                    pool.wait_ge(xn_in[jb], 16 * (j // 2 + 1))
                    pool.wait_ge(row_ready, 2)
                    nc.gpsimd.tensor_tensor(xn[jb][:], xn[jb][:], a1[:], ALU.mult).then_inc(xq_done, 1)
                    pool.wait_ge(xq_done, j + 1)
                    nc.gpsimd.tensor_tensor(xn[jb][:], xn[jb][:], b1[:], ALU.add).then_inc(xb_done, 1)
                    pool.wait_ge(ve_done, j + 1)
                    if in_loop(j, 1):
                        pool.wait_ge(n_done, j)
                    nc.gpsimd.tensor_tensor(rstd[:], ve[:], k.negh[:, 0:1], ALU.pow).then_inc(rstd_done, 1)

            loop(pool, step, 1)

        @block.scalar
        def _(act):
            def step(i, b):
                if in_loop(i, 0, TT):
                    act.wait_ge(ya_in[b], 16 * (i // 2 + 1))
                    act.wait_ge(cols, 4 * (i + 1))
                    if in_loop(i, 2):
                        act.wait_ge(r_done, i - 1)
                    nc.scalar.activation(m[b][:], ya[b][:], ACT.Copy, scale=ga[b][:]).then_inc(mg_done, 1)
                j, jb = i - 1, 1 - b
                if in_loop(j, 0, TT):
                    act.wait_ge(nmr_done, j + 1)
                    nc.scalar.activation(r[jb][:], r[jb][:], ACT.Identity, bias=nmr[:], scale=rstd[:]
                                         ).then_inc(n_done, 1)

            loop(act, step, 1)

        @block.vector
        def _(dve):
            dve.wait_ge(row_in, 64)
            for row in (a1, b1):
                nc.vector.tensor_scalar(row[:], row[:], ALPHA, None, ALU.mult).then_inc(row_ready, 1)

            def step(i, b):
                if in_loop(i, 0, TT):
                    dve.wait_ge(mg_done, i + 1)
                    dve.wait_ge(yb_in[b], 16 * (i // 2 + 1))
                    nc.vector.scalar_tensor_tensor(out=m[b][:], in0=yb[b][:], scalar=gb[b][:], in1=m[b][:],
                                                   op0=ALU.mult, op1=ALU.add).then_inc(ms_done, 1)
                    dve.wait_ge(ms_done, i + 1)
                    nc.vector.tensor_tensor(m[b][:], m[b][:], k.g2[:], ALU.mult).then_inc(mm_done, 1)
                    dve.wait_ge(mm_done, i + 1)
                    dve.wait_ge(xb_done, i + 1)
                    if in_loop(i, 2):
                        dve.wait_ge(og_done, i - 1)
                    nc.vector.tensor_tensor(r[b][:], m[b][:], xn[b][:], ALU.add).then_inc(r_done, 1)
                    dve.wait_ge(r_done, i + 1)
                    for n in range(2):
                        nc.vector.bn_stats(bst[:, n, :], r[b][:, n * 512:(n + 1) * 512]).then_inc(bn_done, 1)
                    dve.wait_ge(bn_done, 2 * (i + 1))
                    dve.sem_inc(k.passed, 1)
                    nc.vector.bn_aggr(mv[:], bst[:].rearrange("p a b -> p (a b)")).then_inc(mv_done, 1)
                    dve.wait_ge(mv_done, i + 1)
                    nc.vector.tensor_scalar(ve[:], mv[:, 1:2], EPS, None, ALU.add).then_inc(ve_done, 1)
                    dve.wait_ge(rstd_done, i + 1)
                    if in_loop(i, 1):
                        dve.wait_ge(n_done, i)
                    nc.vector.scalar_tensor_tensor(out=nmr[:], in0=mv[:, 0:1], scalar=-1.0, in1=rstd[:],
                                                   op0=ALU.mult, op1=ALU.mult).then_inc(nmr_done, 1)
                    dve.wait_ge(n_done, i + 1)
                    if in_loop(i, 2):
                        dve.wait_ge(stored[b], 16 * (i // 2))
                    nc.vector.tensor_tensor(o[b][:], r[b][:], lng[:], ALU.mult).then_inc(og_done, 1)
                    dve.wait_ge(og_done, i + 1)
                    nc.vector.tensor_tensor(o[b][:], o[b][:], lnb[:], ALU.add).then_inc(o_done, 1)

            loop(dve, step)


class Kit:

    def __init__(self, nc, d, ctx):
        self.nc, self.d, self.ctx = nc, d, ctx
        self.used, self.semaphores = [], ctx

        def scratch(name, shape, dt=F32):
            return nc.dram_tensor(name, shape, dt, kind="Internal").ap()

        self.hmd = scratch("hm_parts", (NC_, P, 2 * KK * CHUNK))
        self.acd = scratch("acum_rows", (STEPS * 2 * RH, P))
        self.ytd = scratch("y_t", (TT, P, YTILES, P))
        self.xnd = scratch("xn", (TT, P, D))
        self.h2d = scratch("hm2", (SEQ, D))
        self.slotd = scratch("token_by_slot", ((MAXT + 1) * P, 1))
        self.ysd = scratch("expert_out", (MAXT * P, D))
        sb, _, sem = self.makers(ctx)
        self.ident = sb("ident", [P, P])
        self.ones = sb("ones", [P, P])
        self.mask3 = sb("mask3", [P, 3 * P])
        self.below = sb("below", [P, P])
        self.keep = sb("keep", [P, STEPS + 2])
        self.negh = sb("negh", [P, 2])
        self.eps = sb("eps", [P, 2])
        self.eidx = sb("eidx", [P, EPG])
        self.tidx = sb("tidx", [P, MAXT])
        self.tok = sb("tok", [P, TT])
        self.eidx_i = sb("eidx_i", [P, EPG], I32)
        self.tidx_i = sb("tidx_i", [P, MAXT], I32)
        self.tok_i = sb("tok_i", [P, TT], I32)
        self.cs = sb("cs", [P, KK])
        self.par = sb("par", [P, GROUPS, CONV * (TAPS + 1)])
        self.drow = sb("drow", [P, HEADS])
        self.const_set = sem("const_set")
        self.passed = sem("passed")

    def later(self):
        sb, _, _ = self.makers(self.ctx)
        self.g2 = sb("g2", [P, D])
        self.gate_a, self.gate_b = sb("gate_a", [P, TT]), sb("gate_b", [P, TT])
        self.slot_a, self.slot_b = sb("slot_a", [P, TT], I32), sb("slot_b", [P, TT], I32)
        self.tile_expert = sb("tile_expert", [P, MAXT], I32)
        self.last_pair = sb("last_pair", [P, 1], I32)
        self.ids = sb("ids", [P, MAXT + 1], I32)

    def makers(self, ctx):
        nc = self.nc
        return (lambda name, shape, dt=F32: ctx.enter_context(nc.sbuf_tensor(name, shape, dt)),
                lambda name, shape: ctx.enter_context(nc.psum_tensor(name, shape, F32)),
                self.semaphore)

    def semaphore(self, name):
        self.used.append(self.semaphores.enter_context(self.nc.semaphore(name)))
        return self.used[-1]


def program(nc, d, out, stop=9):
    with ExitStack() as ctx:
        k = Kit(nc, d, ctx)
        with ExitStack() as ctx1:
            k.ctx1 = ctx1
            constants(nc, k)
        with ExitStack() as ctx1:
            sb, _, _ = k.makers(ctx1)
            k.nwrow = sb("nwrow", [P, DI])
            k.tab = sb("tab", [P, 3, STEPS * 2 * RH])
            stage(nc, k, modulated_input)
            if stop > 0:
                stage(nc, k, mixer_steps)
        k.later()
        if stop > 1:
            with ExitStack() as ctx2:
                sb, ps, _ = k.makers(ctx2)
                lgP = ps("lgP", [P, TT * EXPERTS])
                with ExitStack() as ctx3:
                    sb, ps, _ = k.makers(ctx3)
                    k.g1, k.a2, k.b2 = sb("g1", [P, D]), sb("a2", [P, D]), sb("b2", [P, D])
                    w_hi, w_lo = sb("wo_hi", [P, YTILES, D], F32R), sb("wo_lo", [P, YTILES, D], F32R)
                    stage(nc, k, row_vectors, w_hi, w_lo)
                    stage(nc, k, out_projection, w_hi, w_lo, lgP)
                if stop > 2:
                    stage(nc, k, route, lgP)
        if stop > 3:
            stage(nc, k, experts)
        if stop > 4:
            stage(nc, k, output, out)
    return k


def laid_out(inputs):
    import numpy as np
    a = {n: np.asarray(v) for n, v in inputs.items()}
    cw, cb = a["ssm_conv_w"][0], a["ssm_conv_b"][0]
    wb = np.concatenate([cw, cb[None]], 0)
    xs = wb[:, :DI].reshape(5, GROUPS, 2, P)
    bs = wb[:, DI:DI + GROUPS * STATE].reshape(5, GROUPS, 1, P)
    cc = wb[:, DI + GROUPS * STATE:].reshape(5, GROUPS, 1, P)
    par = np.concatenate([xs, bs, cc], 2).transpose(3, 1, 2, 0).reshape(P, GROUPS, CONV * 5)
    r = {
        "x": a["x"][0], "c_cols": a["c"].reshape(KK, P).T, "w_ada": a["w_ada"][0],
        "b_ada_cols": a["b_ada"][0, :2 * D].reshape(16, P).T, "b_ada": a["b_ada"],
        "ln_g": a["ln_g"][0], "ln_b": a["ln_b"][0], "w_in": a["ssm_w_in"][0], "conv_par": par,
        "dt_bias": a["ssm_dt_bias"][0], "a_log": a["ssm_a_log"][0], "d_skip": a["ssm_d"][0],
        "norm_w": a["ssm_norm_w"][0], "w_out": a["ssm_w_out"][0], "w_router": a["w_router"],
        "b_router": a["b_router"], "w_gate": a["moe_w_gate"][0], "w_up": a["moe_w_up"][0],
        "w_down": a["moe_w_down"][0],
    }
    return {n: np.ascontiguousarray(v) for n, v in r.items()}


def kernel(**inputs):
    import numpy as _np
    import concourse.bacc as _bacc
    from concourse.bass_utils import run_bass_kernel_spmd as _run

    nc = _bacc.Bacc("TRN2", target_bir_lowering=False, num_devices=1)
    arrays, d = {}, {}
    for name, a in laid_out(inputs).items():
        arrays[f"in_{name}"] = a
        d[name] = nc.dram_tensor(f"in_{name}", a.shape, mybir.dt.from_np(a.dtype), kind="ExternalInput").ap()
    out = nc.dram_tensor("out", (SEQ, D), F32, kind="ExternalOutput").ap()
    program(nc, d, out)
    r = _run(nc, [arrays], core_ids=[0])
    return _np.asarray(r.results[0]["out"]).reshape(1, SEQ, D)
```

```python
from contextlib import ExitStack

import concourse.bass as bass
from concourse import mybir

F32 = mybir.dt.float32
F32R = mybir.dt.float32r
I32 = mybir.dt.int32
ALU = mybir.AluOpType
ACT = mybir.ActivationFunctionType
AX = mybir.AxisListType

P = 128
D = 1024
SEQ = 2048
KK = D // P
TT = SEQ // P
DI = 2048
GROUPS = 8
STATE = 128
HEADS = 32
RH = HEADS // GROUPS
HD = 64
GW = RH * HD
CHUNK = 256
NC_ = SEQ // CHUNK
STEPS = GROUPS * NC_
XBC = DI
COL_B = XBC + DI
COL_C = COL_B + GROUPS * STATE
COL_DT = COL_C + GROUPS * STATE
TAPS = 4
CONV = 4
PARTS = CONV + 1
EXPERTS = 32
EGROUPS = 4
EPG = EXPERTS // EGROUPS
FE = 512
ALPHA = 2.0 ** 0.25
EPS = 1e-5
MAXT = 64
NTAB = MAXT + 2
YTILES = DI // P


def in_loop(i, low=0, high=STEPS):
    return not isinstance(i, int) or low <= i < high


def constants(nc, k, ctx):
    block = ctx.enter_context(nc.Block())

    @block.gpsimd
    def _(pool):
        nc.gpsimd.memset(k.ident[:], 0.0).then_inc(k.const_set, 1)
        nc.gpsimd.memset(k.ones[:], 1.0).then_inc(k.const_set, 1)
        nc.gpsimd.memset(k.mask3[:], 1.0).then_inc(k.const_set, 1)
        nc.gpsimd.memset(k.below[:], 1.0).then_inc(k.const_set, 1)
        nc.gpsimd.memset(k.keep[:], 1.0).then_inc(k.const_set, 1)
        nc.gpsimd.memset(k.negh[:], -0.5).then_inc(k.const_set, 1)
        nc.gpsimd.iota(k.eidx_i[:], pattern=[[1, EPG]], base=0, channel_multiplier=0).then_inc(k.const_set, 1)
        nc.gpsimd.iota(k.tidx_i[:], pattern=[[1, NTAB]], base=0, channel_multiplier=0).then_inc(k.const_set, 1)
        nc.gpsimd.iota(k.tok_i[:], pattern=[[P, TT]], base=0, channel_multiplier=1).then_inc(k.const_set, 1)
        nc.gpsimd.memset(k.eps[:], EPS).then_inc(k.const_set, 1)
        pool.wait_ge(k.const_set, 10)
        nc.gpsimd.affine_select(out=k.ident[:], in_=k.ident[:], compare_op=ALU.not_equal, fill=1.0, base=0,
                                pattern=[[-1, P]], channel_multiplier=1).then_inc(k.const_set, 1)
        for q in (0, 2):
            nc.gpsimd.affine_select(out=k.mask3[:, q * P:(q + 1) * P], in_=k.mask3[:, q * P:(q + 1) * P],
                                    compare_op=ALU.is_ge, fill=0.0, base=0, pattern=[[1, P]],
                                    channel_multiplier=-1).then_inc(k.const_set, 1)
        nc.gpsimd.affine_select(out=k.below[:], in_=k.below[:], compare_op=ALU.is_gt, fill=0.0, base=0,
                                pattern=[[1, P]], channel_multiplier=-1).then_inc(k.const_set, 1)
        nc.gpsimd.memset(k.keep[:, 0:STEPS + 1:NC_], 0.0).then_inc(k.const_set, 1)
        nc.gpsimd.tensor_copy(k.eidx[:], k.eidx_i[:]).then_inc(k.const_set, 1)
        nc.gpsimd.tensor_copy(k.tidx[:], k.tidx_i[:]).then_inc(k.const_set, 1)
        nc.gpsimd.tensor_copy(k.tok[:], k.tok_i[:]).then_inc(k.const_set, 1)
        pool.wait_ge(k.const_set, 18)


def clear_semaphores(nc, k):
    with nc.Block() as block:

        @block.gpsimd
        def _(pool):
            for s in k.used:
                pool.sem_clear(s)


def stage(nc, k, build, *args):
    with ExitStack() as semaphores:
        k.used, k.semaphores = [], semaphores
        build(nc, k, *args)
        clear_semaphores(nc, k)


def modulated_input(nc, k):
    with ExitStack() as ctx:
        sb, ps, sem = k.makers(ctx)
        NS = 4
        TB = SEQ // 512
        xt = [sb(f"xt{s}", [P, D], F32) for s in range(8)]
        hf = [sb(f"hf{s}", [P, KK, 512], F32) for s in range(2)]
        hl = [sb(f"hl{b}", [P, 2, 2, KK, CHUNK], F32R) for b in range(2)]
        wa = [hl[s // 2][:, s % 2].rearrange("p s (a b) t -> p (s a) (b t)", b=2).bitcast(F32) for s in range(NS)]
        arow = sb("arow", [1, NS * 512])
        dts = sb("dts", [HEADS, 512])
        c_in = sb("c_in", [P, KK], F32)
        c_th = sb("c_th", [P, KK], F32)
        c_half = sb("c_half", [P, KK], F32)
        bcol = sb("bcol", [P, 16], F32)
        mcol = sb("mcol", [P, 16], F32)
        wdt = sb("wdt", [P, KK, HEADS], F32)
        dtb = sb("dtb", [P, HEADS], F32)
        al = sb("al", [P, HEADS], F32)
        v = sb("v", [P, TT * HEADS], F32)
        nv = sb("nv", [P, TT * HEADS], F32)
        e = sb("e", [P, TT * HEADS], F32)
        u = sb("u", [P, TT * HEADS], F32)
        ln = sb("ln", [P, TT * HEADS], F32)
        zr = sb("zr", [P, TT * HEADS], F32)
        dtn = sb("dtn", [P, TT * HEADS], F32)
        dta = sb("dta", [P, TT * HEADS], F32)
        acrow = sb("acrow", [P, 4, P], F32)
        adaP = ps("adaP", [P, 512])
        dtP = ps("dtP", [P, 512])
        acP = ps("acP", [P, 512])
        rowP = ps("rowP", [P, 512])
        ada_rows = (acP, rowP)
        trP = [ps(f"trP{s}", [P, 512]) for s in range(4)]
        small_in, c_act, cs_ready = sem("small_in"), sem("c_act"), sem("cs_ready")
        arow_done, ada_tr, dts_done, dt_tr = sem("arow_done"), sem("ada_tr"), sem("dts_done"), sem("dt_tr")
        wa_in = [sem(f"wa_in{s}") for s in range(NS)]
        x_in = [sem(f"x_in{s}") for s in range(8)]
        ada_mm, mcol_ready = sem("ada_mm"), sem("mcol_ready")
        tr_done, full_ready, hi_ready, lo_ready = (sem(n) for n in ("tr_done", "full_ready", "hi_ready", "lo_ready"))
        hm_out, dt_mm, chain, act_chain, ac_mm = (
            [sem(f"hm_out{b}") for b in range(2)], *(sem(n) for n in ("dt_mm", "chain", "act_chain", "ac_mm")))
        ac_tr, row_ready, row_out, x_used = sem("ac_tr"), sem("row_ready"), sem("row_out"), sem("x_used")
        par_done = sem("par_done")
        block = ctx.enter_context(nc.Block())
        w_ada = k.d["w_ada"].rearrange("(kk p) n -> p kk n", p=P)

        @block.sync
        def _(sp):
            sp.dma_start(c_in[:], k.d["c_cols"]).then_inc(small_in, 16)
            sp.dma_start(bcol[:], k.d["b_ada_cols"]).then_inc(small_in, 16)
            sp.dma_start(k.par[:], k.d["conv_par"]).then_inc(small_in, 16)
            sp.dma_start(dtb[:], k.d["dt_bias"].partition_broadcast(P)).then_inc(small_in, 16)
            sp.dma_start(al[:], k.d["a_log"].partition_broadcast(P)).then_inc(small_in, 16)
            sp.dma_start(k.drow[:], k.d["d_skip"].partition_broadcast(P)).then_inc(small_in, 16)
            sp.dma_start(k.nwrow[:], k.d["norm_w"].partition_broadcast(P)).then_inc(small_in, 16)
            sp.dma_start(wdt[:], k.d["w_in"].rearrange("(kk p) n -> p kk n", p=P)[:, :, COL_DT:COL_DT + HEADS]
                         ).then_inc(small_in, 16)
            for s in range(NS):
                sp.dma_start(wa[s], w_ada[:, :, s * 512:(s + 1) * 512]).then_inc(wa_in[s], 16)
            for tb in range(TB):
                if tb + 2 < TB:
                    sp.wait_ge(x_used, tb + 1)
                    for j in range(4):
                        i = 4 * (tb % 2) + j
                        sp.dma_start(xt[i][:], k.d["x"][(8 + i) * P:(9 + i) * P, :]).then_inc(x_in[i], 16)
                sp.wait_ge(lo_ready, KK * (tb + 1))
                for q in range(2):
                    sp.dma_start(k.hmd[2 * tb + q], hl[tb % 2][:, q].rearrange("p s k t -> p (s k t)").bitcast(F32)
                                 ).then_inc(hm_out[tb % 2], 16)
            for b in range(2):
                sp.wait_ge(hm_out[b], 32 * TB // 2)
            sp.wait_ge(row_ready, 1)
            sp.dma_start(k.acd.rearrange("(q h) t -> h q t", h=P), acrow[:]).then_inc(row_out, 16)
            sp.wait_ge(row_out, 16)

        @block.scalar
        def _(act):
            act.wait_ge(small_in, 16 * 8)
            nc.scalar.activation(c_th[:], c_in[:], ACT.Tanh, scale=0.5).then_inc(c_act, 1)
            act.wait_ge(wa_in[1], 16)
            for t in range(8):
                act.dma_start(xt[t][:], k.d["x"][t * P:(t + 1) * P, :]).then_inc(x_in[t], 16)
            for s in range(NS):
                act.wait_ge(ada_mm, s + 1)
                nc.scalar.copy(arow[:, s * 512:(s + 1) * 512], ada_rows[s % 2][0:1, :]).then_inc(arow_done, 1)
            for tb in range(TB):
                for kk in range(KK):
                    act.wait_ge(full_ready, KK * tb + kk + 1)
                    if kk == 0 and tb >= 2:
                        act.wait_ge(hm_out[tb % 2], 32 * (tb // 2))
                    nc.scalar.copy(hl[tb % 2][:, :, 0, kk, :], hf[tb % 2][:, kk, :].rearrange("p (c t) -> p c t", c=2)
                                   ).then_inc(hi_ready, 1)
                act.wait_ge(dt_mm, tb + 1)
                if tb:
                    act.wait_ge(dt_tr, tb)
                nc.scalar.copy(dts[:], dtP[0:HEADS, :]).then_inc(dts_done, 1)
            act.wait_ge(chain, 5)
            nc.scalar.activation(e[:], nv[:], ACT.Exp).then_inc(act_chain, 1)
            nc.scalar.activation(al[:], al[:], ACT.Exp).then_inc(act_chain, 1)
            act.wait_ge(chain, 6)
            nc.scalar.activation(ln[:], u[:], ACT.Ln).then_inc(act_chain, 1)
            act.wait_ge(chain, 16)
            nc.scalar.activation(k.tab[:, 2, :], k.tab[:, 1, :], ACT.Exp).then_inc(act_chain, 1)
            act.wait_ge(ac_tr, 1)
            nc.scalar.copy(acrow[:].rearrange("p q t -> p (q t)"), rowP[:]).then_inc(row_ready, 1)

        @block.tensor
        def _(pe):
            pe.wait_ge(cs_ready, 1)
            for s in range(NS):
                pe.wait_ge(wa_in[s], 16)
                if s >= 2:
                    pe.wait_ge(arow_done, s - 1)
                for kk in range(KK):
                    mm = nc.tensor.matmul(ada_rows[s % 2][0:1, :], k.cs[:, kk:kk + 1], wa[s][:, kk, :],
                                          start=kk == 0, stop=kk == KK - 1)
                mm.then_inc(ada_mm, 1)
            pe.wait_ge(arow_done, NS)
            for j in range(16):
                tr = nc.tensor.transpose(adaP[:, j:j + 1], arow[:, j * P:(j + 1) * P], k.ident[0:1, 0:1])
            tr.then_inc(ada_tr, 1)

            def dt_product(tb, kk):
                pe.wait_ge(full_ready, KK * tb + kk + 1)
                if kk == 0 and tb:
                    pe.wait_ge(dts_done, tb)
                mm = nc.tensor.matmul(dtP[0:HEADS, :], wdt[:, kk, :], hf[tb % 2][:, kk, :],
                                      start=kk == 0, stop=kk == KK - 1)
                if kk == KK - 1:
                    mm.then_inc(dt_mm, 1)

            for tb in range(TB):
                for j in range(4):
                    pe.wait_ge(x_in[4 * (tb % 2) + j], 16 * (tb // 2 + 1))
                for kk in range(KK):
                    if kk >= 4 or tb:
                        pe.wait_ge(full_ready, KK * tb + kk - 3)
                    for j in range(4):
                        tr = nc.tensor.transpose(trP[kk % 4][:, j * P:(j + 1) * P],
                                                 xt[4 * (tb % 2) + j][:, kk * P:(kk + 1) * P], k.ident[:])
                    tr.then_inc(tr_done, 1)
                    if kk >= 2:
                        dt_product(tb, kk - 2)
                pe.wait_ge(tr_done, KK * (tb + 1))
                pe.sem_inc(x_used, 1)
                for kk in range(KK - 2, KK):
                    dt_product(tb, kk)
                pe.wait_ge(dts_done, tb + 1)
                for j in range(4):
                    tr = nc.tensor.transpose(adaP[:, (4 * tb + j) * HEADS:(4 * tb + j + 1) * HEADS],
                                             dts[:, j * P:(j + 1) * P], k.ident[0:HEADS, 0:HEADS])
                tr.then_inc(dt_tr, 1)
            pe.wait_ge(chain, 14)
            nc.tensor.matmul(acP[:], k.mask3[:, 0:P], dta[:], start=True, stop=False, skip_group_check=True)
            nc.tensor.matmul(acP[:].rearrange("p (c a h) -> p a c h", c=NC_, a=2)[:, 1], k.ones[:, 0:P],
                             dta[:].rearrange("p (c a h) -> p a c h", c=NC_, a=2)[:, 0],
                             start=False, stop=True, skip_group_check=True).then_inc(ac_mm, 1)
            pe.wait_ge(chain, 16)
            for q in range(4):
                tr = nc.tensor.transpose(rowP[:, q * P:(q + 1) * P], k.tab[:, 1, q * P:(q + 1) * P], k.ident[:])
            tr.then_inc(ac_tr, 1)

        @block.vector
        def _(dve):
            count = [0]

            def link(ins):
                count[0] += 1
                ins.then_inc(chain, 1)
                dve.wait_ge(chain, count[0])

            dve.wait_ge(small_in, 16 * 8)
            nc.vector.tensor_scalar(k.par[:], k.par[:], 0.5, None, ALU.mult).then_inc(par_done, 1)
            nc.vector.tensor_scalar(k.nwrow[:], k.nwrow[:], 0.5, None, ALU.mult).then_inc(par_done, 1)
            link(nc.vector.tensor_scalar(c_half[:], c_in[:], 0.5, None, ALU.mult))
            dve.wait_ge(c_act, 1)
            nc.vector.scalar_tensor_tensor(out=k.cs[:], in0=c_th[:], scalar=1.0, in1=c_half[:], op0=ALU.add,
                                           op1=ALU.mult).then_inc(cs_ready, 1)
            dve.wait_ge(ada_tr, 1)
            link(nc.vector.tensor_tensor(mcol[:], adaP[:, 0:16], bcol[:], ALU.add))
            link(nc.vector.tensor_scalar(mcol[:, 8:16], mcol[:, 8:16], 1.0, None, ALU.add))

            def low_part(tb, kk):
                dve.wait_ge(hi_ready, KK * tb + kk + 1)
                nc.vector.tensor_tensor(hl[tb % 2][:, :, 1, kk, :], hf[tb % 2][:, kk, :].rearrange("p (c t) -> p c t", c=2),
                                        hl[tb % 2][:, :, 0, kk, :].bitcast(F32), ALU.subtract).then_inc(lo_ready, 1)

            for tb in range(TB):
                if tb >= 2:
                    dve.wait_ge(dt_mm, tb - 1)
                    dve.wait_ge(lo_ready, KK * (tb - 1))
                for kk in range(KK):
                    dve.wait_ge(tr_done, KK * tb + kk + 1)
                    nc.vector.tensor_scalar(hf[tb % 2][:, kk, :], trP[kk % 4][:], mcol[:, 8 + kk:9 + kk],
                                            mcol[:, kk:kk + 1], ALU.mult, ALU.add).then_inc(full_ready, 1)
                    if kk >= 1:
                        low_part(tb, kk - 1)
                low_part(tb, KK - 1)
            dve.wait_ge(dt_tr, TB)
            vh = v[:].rearrange("p (t h) -> p t h", h=HEADS)
            link(nc.vector.tensor_tensor(vh, adaP[:].rearrange("p (t h) -> p t h", h=HEADS),
                                         dtb[:].unsqueeze(1).to_broadcast([P, TT, HEADS]), ALU.add))
            link(nc.vector.scalar_tensor_tensor(out=nv[:], in0=v[:], scalar=-1.0, in1=v[:], op0=ALU.mult, op1=ALU.min))
            dve.wait_ge(act_chain, 1)
            link(nc.vector.tensor_scalar(u[:], e[:], 1.0, None, ALU.add))
            link(nc.vector.tensor_scalar(nv[:], u[:], -1.0, None, ALU.add))
            link(nc.vector.tensor_scalar(zr[:], nv[:], 0.0, None, ALU.is_equal))
            link(nc.vector.tensor_scalar(nv[:], nv[:], 1e-30, None, ALU.max))
            link(nc.vector.reciprocal(nv[:], nv[:]))
            dve.wait_ge(act_chain, 3)
            link(nc.vector.tensor_tensor(nv[:], nv[:], ln[:], ALU.mult))
            link(nc.vector.tensor_tensor(nv[:], nv[:], zr[:], ALU.add))
            link(nc.vector.tensor_tensor(nv[:], nv[:], e[:], ALU.mult))
            dtg = "p (c a g r) -> p a c g r"
            tabg = "p (g c a r) -> p a c g r"
            n = count[0]
            nc.vector.scalar_tensor_tensor(out=dtn[:], in0=v[:], scalar=0.0, in1=nv[:], op0=ALU.max,
                                           op1=ALU.add).then_inc(par_done, 1)
            dve.wait_ge(par_done, 3)
            nc.vector.scalar_tensor_tensor(out=dta[:].rearrange("p (t h) -> p t h", h=HEADS),
                                           in0=dtn[:].rearrange("p (t h) -> p t h", h=HEADS), scalar=-1.0,
                                           in1=al[:].unsqueeze(1).to_broadcast([P, TT, HEADS]), op0=ALU.mult,
                                           op1=ALU.mult).then_inc(chain, 14 - n)
            count[0] = 14
            for a in range(2):
                nc.vector.tensor_copy(k.tab[:, 0, :].rearrange(tabg, g=GROUPS, c=NC_, a=2)[:, a],
                                      dtn[:].rearrange(dtg, c=NC_, a=2, g=GROUPS)[:, a]).then_inc(par_done, 1)
            dve.wait_ge(ac_mm, 1)
            for a in range(2):
                nc.vector.tensor_copy(k.tab[:, 1, :].rearrange(tabg, g=GROUPS, c=NC_, a=2)[:, a],
                                      acP[:].rearrange(dtg, c=NC_, a=2, g=GROUPS)[:, a]).then_inc(chain, 1)
            dve.wait_ge(chain, 16)
            dve.wait_ge(act_chain, 4)


def by_group(eng, step):
    for c in range(NC_):
        step(c, c % 2, last=c == NC_ - 1)
    with eng.Fori(1, GROUPS - 1) as g:
        step(NC_ * g, 0, first=True)
        step(NC_ * g + 1, 1)
        with eng.Fori(1, NC_ // 2 - 1) as h:
            step(NC_ * g + 2 * h, 0)
            step(NC_ * g + 2 * h + 1, 1)
        step(NC_ * g + NC_ - 2, 0)
        step(NC_ * g + NC_ - 1, 1, last=True)
    start = NC_ * (GROUPS - 1)
    step(start, 0, first=True)
    step(start + 1, 1)
    with eng.Fori(1, NC_ // 2) as h:
        step(start + 2 * h, 0)
        step(start + 2 * h + 1, 1)
    step(STEPS, 0)
    step(STEPS + 1, 1)


def mixer_steps(nc, k):
    with ExitStack() as ctx:
        sb, ps, sem = k.makers(ctx)
        wide = [P] * CONV + [GW]
        w_raw = [sb(f"w_raw{m}", [P, KK, wide[m]]) for m in range(PARTS)]
        w_hi = [sb(f"w_hi{m}", [P, KK, wide[m]], F32R) for m in range(PARTS)]
        w_lo = [sb(f"w_lo{m}", [P, KK, wide[m]], F32R) for m in range(PARTS)]
        hm = [sb(f"hm{b}", [P, 2, KK, CHUNK], F32R) for b in range(2)]
        zero = sb("zero_rows", [P, CHUNK])
        zero_set, zero_out = sem("zero_set"), sem("zero_out")
        acb = [sb(f"acb{b}", [P, 2, RH, P]) for b in range(2)]
        parb = [sb(f"parb{b}", [P, CONV, TAPS + 1]) for b in range(2)]
        tb = [sb(f"tb{b}", [P, 3, 2, RH]) for b in range(2)]
        ub = [sb(f"ub{b}", [P, CONV, CHUNK + TAPS - 1]) for b in range(2)]
        cv = [sb(f"cv{b}", [P, CONV, CHUNK]) for b in range(2)]
        th = sb("th", [P, CONV, CHUNK])
        xbc = [sb(f"xbc{b}", [P, CONV, CHUNK]) for b in range(2)]
        xs = sb("xs", [P, 2, GW])
        bs = sb("bs", [P, 2, P])
        zth = sb("zth", [P, 2, GW])
        zs = [sb(f"zs{b}", [P, 2, GW]) for b in range(2)]
        seg0, seg1 = sb("seg0", [P, RH, CHUNK]), sb("seg1", [P, RH, P])
        gm = sb("gm", [P, 3 * P])
        wt0, wt1 = sb("wt0", [P, RH, CHUNK]), sb("wt1", [P, RH, P])
        te = sb("te", [P, 2, RH])
        el = sb("el", [P, RH])
        ek = sb("ek", [P, RH])
        xdt, xend, xd = (sb(n, [P, 2, GW]) for n in ("xdt", "xend", "xd"))
        st, stt = sb("st", [P, GW]), sb("stt", [P, GW])
        t1, y, gt, gw, yn = (sb(n, [P, 2, GW]) for n in ("t1", "y", "gt", "gw", "yn"))
        sq = sb("sq", [P, 2, GW])
        ss, ms, rs = sb("ss", [P, 2]), sb("ms", [P, 2]), sb("rs", [P, 2])
        yt = [sb(f"yt{b}", [P, 2, 2, P]) for b in range(2)]
        pj = [ps(f"pj{b}", [P, 512]) for b in range(3)]
        tx, gp, yi, yx, sbp = (ps(n, [P, 512]) for n in ("tx", "gp", "yi", "yx", "sbp"))

        w_in_s = [sem(f"w_in_s{m}") for m in range(PARTS)]
        w_hi_s = sem("w_hi_s")
        w_split = [sem(f"w_split{m}") for m in range(PARTS)]
        hm_in = [sem(f"hm_in{b}") for b in range(2)]
        ac_in = [sem(f"ac_in{b}") for b in range(2)]
        y_stored = [sem(f"y_stored{b}") for b in range(2)]
        (proj_done, conv_out, z_out, par_ready, halo_done, conv_tap, th_done, silu_done, xs_tr, b_tr, g_done,
         xs_out, b_out, zth_done, seg_done, exp_done, el_done, te_done, ek_done, gm_done, w_done,
         x_done, y_mm, st_mm, stt_done, st_done, t1_done, y_done, y3_done, gt_done, gw_done, sq_done, ms_done,
         rs_done, yn_done, yt_tr, yt_out, ub_out) = (sem(n) for n in (
             "proj_done conv_out z_out par_ready halo_done conv_tap th_done silu_done xs_tr b_tr g_done "
             "xs_out b_out zth_done seg_done exp_done el_done te_done ek_done gm_done w_done "
             "x_done y_mm st_mm stt_done st_done t1_done y_done y3_done gt_done gw_done sq_done ms_done "
             "rs_done yn_done yt_tr yt_out ub_out").split())
        block = ctx.enter_context(nc.Block())
        w_cols = k.d["w_in"].rearrange("(kk p) n -> p kk n", p=P)

        @block.sync
        def _(sp):
            def weights(g):
                for m, (base, width) in enumerate(((XBC, GW), (XBC + P, GW), (COL_B, STATE), (COL_C, STATE),
                                                   (0, GW))):
                    if in_loop(g, 1, GROUPS):
                        sp.wait_ge(w_split[m], g)
                        sp.sem_inc(k.passed, 1)
                    sp.dma_start(w_raw[m][:], w_cols[:, :, bass.ds(g * width + base, wide[m])]
                                 ).then_inc(w_in_s[m], 16)

            def step(i, b):
                if in_loop(i, 2):
                    sp.wait_ge(proj_done, 6 * (i - 1))
                sp.dma_start(hm[b][:].rearrange("p s k t -> p (s k t)").bitcast(F32),
                             k.hmd[bass.ds(i % NC_, 1)]
                             .rearrange("a p n -> (a p) n")).then_inc(hm_in[b], 16)
                if in_loop(i, 2):
                    sp.wait_ge(seg_done, 8 * (i - 1))
                    sp.wait_ge(el_done, i - 1)
                sp.dma_start(acb[b][:].rearrange("p a r t -> p (a r t)"),
                             k.acd.rearrange("(i n) t -> i (n t)", i=STEPS)[bass.ds(i, 1), :]
                             .rearrange("a n -> (a n)").partition_broadcast(P)).then_inc(ac_in[b], 16)

            def clear(g):
                n = MAXT // 2 // GROUPS
                sp.dma_start(k.ysd[bass.ds((MAXT // 2 + n * g) * P, n * P), :]
                             .rearrange("(p t) (q n) -> p (t q) n", p=P, n=CHUNK),
                             zero[:].unsqueeze(1).to_broadcast([P, n * D // CHUNK, CHUNK])).then_inc(zero_out, 16)

            weights(0)
            for c in range(4):
                step(c, c % 2)
            weights(1)
            sp.wait_ge(zero_set, 1)
            clear(0)
            for c in range(4, 8):
                step(c, c % 2)
            with sp.Fori(1, GROUPS - 1) as g:
                for c in range(4):
                    step(g * NC_ + c, c % 2)
                weights(g + 1)
                clear(g)
                for c in range(4, 8):
                    step(g * NC_ + c, c % 2)
            clear(GROUPS - 1)
            for c in range(8):
                step(8 * (GROUPS - 1) + c, c % 2)
            sp.wait_ge(zero_out, 16 * GROUPS)

        @block.gpsimd
        def _(pool):
            def x_products(j):
                xsv = xs[:].rearrange("p a (r q) -> p (a r) q", r=RH)
                pool.wait_ge(xs_out, j + 1)
                if in_loop(j, 1):
                    pool.wait_ge(st_mm, j)
                return xsv

            def tasks(j, b):
                if in_loop(j, 1):
                    gate(j - 1, 1 - b)
                xsv = x_products(j)
                nc.gpsimd.tensor_tensor(xdt[:].rearrange("p a (r q) -> p (a r) q", r=RH), xsv,
                                        tb[b][:, 0].rearrange("p a r -> p (a r)").unsqueeze(2)
                                        .to_broadcast([P, 2 * RH, HD]), ALU.mult).then_inc(x_done, 1)
                for a in range(2):
                    ins = nc.gpsimd.tensor_tensor(
                        xd[:, a].rearrange("p (r q) -> p r q", r=RH), xs[:, a].rearrange("p (r q) -> p r q", r=RH),
                        k.drow[:, bass.ds(RH * (j // NC_), RH)].unsqueeze(2).to_broadcast([P, RH, HD]),
                        ALU.mult)
                    ins.then_inc(x_done, 1)
                pool.wait_ge(te_done, 2 * (j + 1))
                nc.gpsimd.tensor_tensor(xend[:].rearrange("p a (r q) -> p (a r) q", r=RH), xsv,
                                        te[:].rearrange("p a r -> p (a r)").unsqueeze(2)
                                        .to_broadcast([P, 2 * RH, HD]), ALU.mult).then_inc(x_done, 1)

            def gate(j, b):
                pool.wait_ge(y_done, j + 1)
                pool.wait_ge(x_done, 4 * j + 3)
                nc.gpsimd.tensor_tensor(xd[:], y[:], xd[:], ALU.add).then_inc(y3_done, 1)
                pool.wait_ge(y3_done, j + 1)
                pool.wait_ge(z_out, 2 * (j + 1))
                if in_loop(j, 1):
                    pool.wait_ge(sq_done, 2 * j)
                nc.gpsimd.tensor_tensor(gt[:], xd[:], zs[b][:], ALU.mult).then_inc(gt_done, 1)
                pool.wait_ge(gt_done, j + 1)
                if in_loop(j, 1):
                    pool.wait_ge(yn_done, 2 * j)
                for a in range(2):
                    nc.gpsimd.tensor_tensor(gw[:, a], gt[:, a],
                                            k.nwrow[:, bass.ds(GW * (j // NC_), GW)], ALU.mult
                                            ).then_inc(gw_done, 1)
                pool.wait_ge(sq_done, 2 * (j + 1))
                nc.gpsimd.tensor_tensor(ms[:], ss[:], k.eps[:], ALU.add).then_inc(ms_done, 1)
                pool.wait_ge(ms_done, j + 1)
                nc.gpsimd.tensor_tensor(rs[:], ms[:], k.negh[:], ALU.pow).then_inc(rs_done, 1)

            nc.gpsimd.memset(zero[:], 0.0).then_inc(zero_set, 1)
            tasks(0, 0)
            tasks(1, 1)
            with pool.Fori(1, STEPS // 2) as h:
                tasks(2 * h, 0)
                tasks(2 * h + 1, 1)
            gate(STEPS - 1, 1)

        @block.tensor
        def _(pe):
            def proj(i, b, m):
                if m == 0:
                    pe.wait_ge(hm_in[b], 16 * (i // 2 + 1))
                pe.wait_ge(w_split[m], i // NC_ + 1)
                if m == 3:
                    pe.wait_ge(conv_out, CONV * i + 1)
                elif in_loop(i, 1):
                    if m == 0:
                        pe.wait_ge(conv_out, CONV * i)
                    else:
                        pe.wait_ge(z_out, 2 * i + m - 2)
                n = 0
                for wp, hp in ((w_hi, 0), (w_hi, 1), (w_lo, 0)):
                    for kk in range(KK):
                        mm = nc.tensor.matmul(pj[m % 3][:, 0:CHUNK], wp[m][:, kk, :], hm[b][:, hp, kk, :],
                                              start=n == 0, stop=n == 3 * KK - 1)
                        n += 1
                mm.then_inc(proj_done, 1)

            def proj_z(i, b, a):
                pe.wait_ge(w_split[CONV], i // NC_ + 1)
                pe.wait_ge(conv_out, CONV * i + 2 + a)
                n = 0
                for wp, hp in ((w_hi, 0), (w_lo, 0), (w_hi, 1)):
                    for kk in range(KK):
                        mm = nc.tensor.matmul(pj[1 + a][:, 0:GW], hm[b][:, hp, kk, a * P:(a + 1) * P],
                                              wp[CONV][:, kk, :], start=n == 0, stop=n == 3 * KK - 1)
                        n += 1
                mm.then_inc(proj_done, 1)

            def step(i, b):
                j, jb = i - 1, 1 - b
                if in_loop(i):
                    for m in range(CONV):
                        proj(i, b, m)
                if in_loop(j):
                    pe.wait_ge(silu_done, j + 1)
                    if in_loop(j, 2):
                        pe.wait_ge(yt_out, j - 1)
                    for m in range(2):
                        for a in range(2):
                            tr = nc.tensor.transpose(tx[:, a * GW + m * P:a * GW + (m + 1) * P],
                                                     xbc[jb][:, m, a * P:(a + 1) * P], k.ident[:])
                    tr.then_inc(xs_tr, 1)
                    pe.wait_ge(st_done, j + 1)
                    for a in range(2):
                        tr = nc.tensor.transpose(sbp[:, a * P:(a + 1) * P], xbc[jb][:, 2, a * P:(a + 1) * P], k.ident[:])
                    tr.then_inc(b_tr, 1)
                    if in_loop(j, 1):
                        pe.wait_ge(gm_done, j)
                    nc.tensor.matmul(gp[:, 0:CHUNK], xbc[jb][:, 2, 0:P], xbc[jb][:, 3, :], start=True, stop=True)
                    nc.tensor.matmul(gp[:, CHUNK:3 * P], xbc[jb][:, 2, P:CHUNK], xbc[jb][:, 3, P:CHUNK],
                                     start=True, stop=True).then_inc(g_done, 1)
                if in_loop(i):
                    for a in range(2):
                        proj_z(i, b, a)
                if in_loop(j):
                    pe.wait_ge(w_done, 2 * (j + 1))
                    pe.wait_ge(x_done, 4 * j + 1)
                    if in_loop(j, 1):
                        pe.wait_ge(y_done, j)
                    for r in range(RH):
                        q = slice(r * HD, (r + 1) * HD)
                        nc.tensor.matmul(yi[:, r * HD:(r + 1) * HD], wt0[:, r, 0:P], xdt[:, 0, q],
                                         start=True, stop=True)
                    for r in range(RH):
                        q = slice(r * HD, (r + 1) * HD)
                        nc.tensor.matmul(yi[:, GW + r * HD:GW + (r + 1) * HD], wt0[:, r, P:CHUNK], xdt[:, 0, q],
                                         start=True, stop=False)
                        nc.tensor.matmul(yi[:, GW + r * HD:GW + (r + 1) * HD], wt1[:, r, :], xdt[:, 1, q],
                                         start=False, stop=True)
                    pe.wait_ge(st_done, j + 1)
                    for a in range(2):
                        mm = nc.tensor.matmul(yx[:, a * GW:(a + 1) * GW], xbc[jb][:, 3, a * P:(a + 1) * P], st[:],
                                              start=True, stop=True)
                    mm.then_inc(y_mm, 1)
                    pe.wait_ge(x_done, 4 * (j + 1))
                    pe.wait_ge(b_out, j + 1)
                    for a in range(2):
                        mm = nc.tensor.matmul(sbp[:, GW:2 * GW], bs[:, a, :], xend[:, a, :],
                                              start=a == 0, stop=a == 1)
                    mm.then_inc(st_mm, 1)
                if in_loop(i - 2):
                    pe.wait_ge(yn_done, 2 * (i - 1))
                    if in_loop(j):
                        pe.wait_ge(xs_out, j + 1)
                    for a in range(2):
                        for m in range(2):
                            tr = nc.tensor.transpose(tx[:, (2 * a + m) * P:(2 * a + m + 1) * P],
                                                     yn[:, a, m * P:(m + 1) * P], k.ident[:])
                    tr.then_inc(yt_tr, 1)

            step(0, 0)
            step(1, 1)
            with pe.Fori(1, STEPS // 2) as h:
                step(2 * h, 0)
                step(2 * h + 1, 1)
            step(STEPS, 0)
            step(STEPS + 1, 1)

        @block.scalar
        def _(act):
            def high(m, n):
                act.wait_ge(w_in_s[m], 16 * (n + 1))
                nc.scalar.copy(w_hi[m][:], w_raw[m][:]).then_inc(w_hi_s, 1)

            def out_conv(i, b, m):
                act.wait_ge(proj_done, 6 * i + m + 1)
                if m == 0:
                    act.wait_ge(par_ready, 2 * i + 1)
                    if in_loop(i, 2):
                        act.wait_ge(silu_done, i - 1)
                    if in_loop(i, 1):
                        act.wait_ge(halo_done, i)
                nc.scalar.copy(ub[b][:, m, TAPS - 1:], pj[m % 3][:, 0:CHUNK]).then_inc(ub_out, 1)
                nc.scalar.activation(cv[b][:, m, :], pj[m % 3][:, 0:CHUNK], ACT.Identity,
                                     bias=parb[b][:, m, TAPS:TAPS + 1], scale=parb[b][:, m, TAPS - 1:TAPS]
                                     ).then_inc(conv_out, 1)

            def exps(j, jb):
                act.wait_ge(seg_done, 8 * j + 8)
                nc.scalar.activation(seg0[:], seg0[:], ACT.Exp).then_inc(exp_done, 1)
                nc.scalar.activation(seg1[:], seg1[:], ACT.Exp).then_inc(exp_done, 1)
                if in_loop(j, 1):
                    act.wait_ge(ek_done, j)
                nc.scalar.activation(el[:], acb[jb][:, 1, :, P - 1], ACT.Exp).then_inc(el_done, 1)

            def step(i, b, first=False, last=False):
                j, jb = i - 1, 1 - b
                if in_loop(i):
                    out_conv(i, b, 0)
                    if last:
                        high(0, i // NC_ + 1)
                    if first:
                        high(CONV, i // NC_)
                if in_loop(i - 2):
                    act.wait_ge(gt_done, i - 1)
                    if in_loop(i - 3):
                        act.wait_ge(ms_done, i - 2)
                    for a in range(2):
                        nc.scalar.activation(sq[:, a], gt[:, a], ACT.Square, scale=0.5 * GW ** -0.5,
                                             accum_out=ss[:, a:a + 1]).then_inc(sq_done, 1)
                if in_loop(j):
                    exps(j, jb)
                if in_loop(i):
                    for m in range(1, CONV):
                        out_conv(i, b, m)
                        if last:
                            high(m, i // NC_ + 1)
                if in_loop(j):
                    act.wait_ge(xs_tr, j + 1)
                    if in_loop(j, 1):
                        act.wait_ge(x_done, 4 * j)
                    nc.scalar.copy(xs[:].rearrange("p a n -> p (a n)"), tx[:]).then_inc(xs_out, 1)
                    act.wait_ge(b_tr, j + 1)
                    if in_loop(j, 1):
                        act.wait_ge(st_mm, j)
                    nc.scalar.copy(bs[:].rearrange("p a n -> p (a n)"), sbp[:, 0:GW]).then_inc(b_out, 1)
                if in_loop(i):
                    for a in range(2):
                        act.wait_ge(proj_done, 6 * i + CONV + a + 1)
                        if in_loop(i, 1):
                            act.wait_ge(z_out, 2 * i + a - 1)
                        nc.scalar.activation(zth[:, a], pj[1 + a][:, 0:GW], ACT.Tanh, scale=0.5
                                             ).then_inc(zth_done, 1)
                    act.wait_ge(conv_tap, 12 * (i + 1))
                    if in_loop(i, 1):
                        act.wait_ge(silu_done, i)
                    nc.scalar.activation(th[:], cv[b][:], ACT.Tanh).then_inc(th_done, 1)
                if in_loop(i - 2):
                    act.wait_ge(yt_tr, i - 1)
                    if in_loop(i - 4):
                        act.wait_ge(y_stored[b], 32 * ((i - 4) // 2 + 1))
                    nc.scalar.copy(yt[b][:].rearrange("p a m t -> p (a m t)"), tx[:]).then_inc(yt_out, 1)
                    act.wait_ge(yt_out, i - 1)
                    c, g = (i - 2) % NC_, (i - 2) // NC_
                    for a in range(2):
                        act.dma_start(k.ytd[bass.ds(2 * c + a, 1), :, bass.ds(2 * g, 2), :]
                                      .rearrange("a p m t -> (a p) m t"), yt[b][:, a]).then_inc(y_stored[b], 16)

            for m in range(PARTS):
                high(m, 0)
            by_group(act, step)
            for b in range(2):
                act.wait_ge(y_stored[b], 16 * STEPS)

        @block.vector
        def _(dve):
            def params(i, b):
                nc.vector.tensor_copy(parb[b][:].rearrange("p m t -> p (m t)"),
                                      k.par[:, bass.ds((i // NC_), 1), :].rearrange("p g n -> p (g n)")
                                      ).then_inc(par_ready, 1)
                nc.vector.tensor_copy(tb[b][:].rearrange("p s a r -> p s (a r)"),
                                      k.tab[:, :, bass.ds(i * 2 * RH, 2 * RH)]).then_inc(par_ready, 1)

            def conv(i, b):
                if isinstance(i, int) and i == 0:
                    nc.vector.memset(ub[b][:, :, 0:TAPS - 1], 0.0).then_inc(halo_done, 1)
                else:
                    dve.wait_ge(ub_out, CONV * i)
                    nc.vector.tensor_scalar(ub[b][:, :, 0:TAPS - 1], ub[1 - b][:, :, CHUNK:CHUNK + TAPS - 1],
                                            k.keep[:, bass.ds(i, 1)], None, ALU.mult).then_inc(halo_done, 1)
                dve.wait_ge(halo_done, i + 1)
                dve.wait_ge(conv_out, CONV * (i + 1))
                for tap in range(TAPS - 1):
                    for m in range(CONV):
                        if tap:
                            dve.wait_ge(conv_tap, 12 * i + CONV * (tap - 1) + m + 1)
                        nc.vector.scalar_tensor_tensor(out=cv[b][:, m, :], in0=ub[b][:, m, tap:tap + CHUNK],
                                                       scalar=parb[b][:, m, tap:tap + 1], in1=cv[b][:, m, :],
                                                       op0=ALU.mult, op1=ALU.add).then_inc(conv_tap, 1)
                for a in range(2):
                    dve.wait_ge(zth_done, 2 * i + a + 1)
                    if in_loop(i, 2) and a == 0:
                        dve.wait_ge(gt_done, i - 1)
                    nc.vector.scalar_tensor_tensor(out=zs[b][:, a], in0=zth[:, a], scalar=1.0,
                                                   in1=pj[1 + a][:, 0:GW], op0=ALU.add, op1=ALU.mult
                                                   ).then_inc(z_out, 1)
                dve.wait_ge(th_done, i + 1)
                if in_loop(i, 2):
                    dve.wait_ge(st_mm, i - 1)
                nc.vector.scalar_tensor_tensor(out=xbc[b][:], in0=th[:], scalar=1.0, in1=cv[b][:], op0=ALU.add,
                                               op1=ALU.mult).then_inc(silu_done, 1)

            def segments(j, b):
                dve.wait_ge(ac_in[b], 16 * (j // 2 + 1))
                dve.wait_ge(par_ready, 2 * (j + 1))
                if in_loop(j, 1):
                    dve.wait_ge(w_done, 2 * j)
                    dve.wait_ge(te_done, 2 * j)
                for r in range(RH):
                    nc.vector.tensor_scalar(seg0[:, r, :].rearrange("p (a t) -> p a t", a=2), acb[b][:, :, r, :],
                                            tb[b][:, 1, 0, r:r + 1], 0.0, ALU.subtract, ALU.min
                                            ).then_inc(seg_done, 1)
                for r in range(RH):
                    nc.vector.tensor_scalar(seg1[:, r, :], acb[b][:, 1, r, :], tb[b][:, 1, 1, r:r + 1], 0.0,
                                            ALU.subtract, ALU.min).then_inc(seg_done, 1)

            def state(j):
                dve.wait_ge(el_done, j + 1)
                nc.vector.tensor_scalar(ek[:], el[:], k.keep[:, bass.ds(j + 1, 1)], None, ALU.mult
                                        ).then_inc(ek_done, 1)
                dve.wait_ge(ek_done, j + 1)
                dve.wait_ge(st_mm, j + 1)
                nc.vector.tensor_tensor(stt[:].rearrange("p (r q) -> p r q", r=RH),
                                        st[:].rearrange("p (r q) -> p r q", r=RH),
                                        ek[:].unsqueeze(2).to_broadcast([P, RH, HD]), ALU.mult
                                        ).then_inc(stt_done, 1)
                dve.wait_ge(stt_done, j + 1)
                nc.vector.scalar_tensor_tensor(out=st[:], in0=sbp[:, GW:2 * GW], scalar=k.keep[:, bass.ds(j + 1, 1)],
                                               in1=stt[:], op0=ALU.mult, op1=ALU.add).then_inc(st_done, 1)

            def combine(j, b):
                dve.wait_ge(y_mm, j + 1)
                nc.vector.tensor_tensor(t1[:].rearrange("p a (r q) -> p (a r) q", r=RH),
                                        yx[:].rearrange("p (n q) -> p n q", q=HD),
                                        tb[b][:, 2].rearrange("p a r -> p (a r)").unsqueeze(2)
                                        .to_broadcast([P, 2 * RH, HD]), ALU.mult).then_inc(t1_done, 1)
                dve.wait_ge(t1_done, j + 1)
                if in_loop(j, 1):
                    dve.wait_ge(y3_done, j)
                nc.vector.tensor_tensor(y[:].rearrange("p a n -> p (a n)"), t1[:].rearrange("p a n -> p (a n)"),
                                        yi[:], ALU.add).then_inc(y_done, 1)

            def weigh(j, b):
                dve.wait_ge(g_done, j + 1)
                nc.vector.tensor_tensor(gm[:], gp[:, 0:3 * P], k.mask3[:], ALU.mult).then_inc(gm_done, 1)
                dve.wait_ge(exp_done, 2 * (j + 1))
                if in_loop(j, 1):
                    dve.wait_ge(x_done, 4 * j)
                nc.vector.tensor_tensor(te[:, 0], seg0[:, :, CHUNK - 1], tb[b][:, 0, 0], ALU.mult).then_inc(te_done, 1)
                nc.vector.tensor_tensor(te[:, 1], seg1[:, :, P - 1], tb[b][:, 0, 1], ALU.mult).then_inc(te_done, 1)
                dve.wait_ge(gm_done, j + 1)
                if in_loop(j, 1):
                    dve.wait_ge(y_mm, j)
                nc.vector.tensor_tensor(wt0[:], seg0[:], gm[:, 0:CHUNK].unsqueeze(1).to_broadcast([P, RH, CHUNK]),
                                        ALU.mult).then_inc(w_done, 1)
                nc.vector.tensor_tensor(wt1[:], seg1[:], gm[:, CHUNK:3 * P].unsqueeze(1).to_broadcast([P, RH, P]),
                                        ALU.mult).then_inc(w_done, 1)

            def low(m, n):
                dve.wait_ge(w_hi_s, PARTS * n + m + 1)
                nc.vector.tensor_tensor(w_lo[m][:], w_raw[m][:], w_hi[m][:].bitcast(F32), ALU.subtract
                                        ).then_inc(w_split[m], 1)

            def step(i, b, first=False, last=False):
                j, jb = i - 1, 1 - b
                if in_loop(i - 2):
                    combine(i - 2, b)
                    state(i - 2)
                if in_loop(i):
                    if in_loop(i, 2):
                        dve.wait_ge(x_done, 4 * (i - 1))
                        dve.wait_ge(t1_done, i - 1)
                    params(i, b)
                if in_loop(j):
                    segments(j, jb)
                if first:
                    low(CONV, i // NC_)
                if in_loop(i - 2):
                    dve.wait_ge(rs_done, i - 1)
                    dve.wait_ge(gw_done, 2 * (i - 1))
                    if in_loop(i - 3):
                        dve.wait_ge(yt_tr, i - 2)
                    for a in range(2):
                        nc.vector.tensor_scalar(yn[:, a], gw[:, a], rs[:, a:a + 1], None, ALU.mult
                                                ).then_inc(yn_done, 1)
                if last:
                    low(0, i // NC_ + 1)
                if in_loop(j):
                    weigh(j, jb)
                if last:
                    for m in range(1, CONV):
                        low(m, i // NC_ + 1)
                if in_loop(i):
                    conv(i, b)

            nc.vector.memset(st[:], 0.0).then_inc(st_done, 1)
            for m in range(PARTS):
                low(m, 0)
            by_group(dve, step)


def row_vectors(nc, k, w_hi, w_lo):
    with ExitStack() as ctx:
        sb, ps, sem = k.makers(ctx)
        NW = 3
        wa = [sb(f"wr{b}", [P, KK, 512]) for b in range(2)]
        wraw = [sb(f"wo_raw{b}", [P, D]) for b in range(NW)]
        csb = sb("csb", [P, KK, P])
        rp = [ps(f"rp{b}", [P, 512]) for b in range(2)]
        rows = [k.g1, k.b2, k.a2]
        NR = 2 * len(rows)
        bias_in, cs_wide, row_mm, row_out, chain = (sem(n) for n in "bias_in cs_wide row_mm row_full chain_r".split())
        wr_in = [sem(f"wr_in{b}") for b in range(2)]
        wo_in = [sem(f"wo_in{b}") for b in range(NW)]
        hi_done, lo_done = sem("wo_hi_done"), sem("wo_lo_done")
        block = ctx.enter_context(nc.Block())
        w_ada = k.d["w_ada"].rearrange("(kk p) n -> p kk n", p=P)

        @block.sync
        def _(sp):
            for n, row in enumerate(rows):
                sp.dma_start(row[:], k.d["b_ada"][0, (2 + n) * D:(3 + n) * D].partition_broadcast(P)
                             ).then_inc(bias_in, 16)
            sp.dma_start(k.a1[:], k.d["ln_g"][0].partition_broadcast(P)).then_inc(bias_in, 16)
            sp.dma_start(k.b1[:], k.d["ln_b"][0].partition_broadcast(P)).then_inc(bias_in, 16)
            for s in range(NR):
                if s >= 2:
                    sp.wait_ge(row_mm, s - 1)
                sp.dma_start(wa[s % 2][:], w_ada[:, :, 2 * D + s * 512:2 * D + (s + 1) * 512]
                             ).then_inc(wr_in[s % 2], 16)

        @block.scalar
        def _(act):
            for m in range(NW):
                act.dma_start(wraw[m][:], k.d["w_out"][m * P:(m + 1) * P, :]).then_inc(wo_in[m], 16)
            for m in range(YTILES):
                act.wait_ge(wo_in[m % NW], 16 * (m // NW + 1))
                nc.scalar.copy(w_hi[:, m, :], wraw[m % NW][:]).then_inc(hi_done, 1)
                n = m - 1 + NW
                if m >= 1 and n < YTILES:
                    act.wait_ge(lo_done, m)
                    act.dma_start(wraw[n % NW][:], k.d["w_out"][n * P:(n + 1) * P, :]).then_inc(wo_in[n % NW], 16)

        @block.tensor
        def _(pe):
            pe.wait_ge(cs_wide, KK)
            for s in range(NR):
                pe.wait_ge(wr_in[s % 2], 16 * (s // 2 + 1))
                if s >= 2:
                    pe.wait_ge(row_out, s - 1)
                for kk in range(KK):
                    mm = nc.tensor.matmul(rp[s % 2][:], csb[:, kk, :], wa[s % 2][:, kk, :],
                                          start=kk == 0, stop=kk == KK - 1)
                mm.then_inc(row_mm, 1)

        @block.vector
        def _(dve):
            for kk in range(KK):
                nc.vector.tensor_scalar(csb[:, kk, :], k.ones[:], k.cs[:, kk:kk + 1], None, ALU.mult
                                        ).then_inc(cs_wide, 1)

            def low(m):
                dve.wait_ge(hi_done, m + 1)
                nc.vector.tensor_tensor(w_lo[:, m, :], wraw[m % NW][:], w_hi[:, m, :].bitcast(F32), ALU.subtract
                                        ).then_inc(lo_done, 1)

            dve.wait_ge(bias_in, 16 * (len(rows) + 2))
            for s in range(NR):
                for m in range(s * YTILES // NR, (s + 1) * YTILES // NR):
                    low(m)
                dve.wait_ge(row_mm, s + 1)
                half = rows[s // 2][:, (s % 2) * 512:(s % 2 + 1) * 512]
                nc.vector.scalar_tensor_tensor(out=half, in0=rp[s % 2][:], scalar=0.0 if s // 2 == 1 else 1.0,
                                               in1=half, op0=ALU.add, op1=ALU.add).then_inc(row_out, 1)
            dve.wait_ge(row_out, NR)
            t = csb[:].rearrange("p k t -> p (k t)")
            nc.vector.tensor_tensor(t, k.a2[:], k.b1[:], ALU.mult).then_inc(chain, 1)
            dve.wait_ge(chain, 1)
            nc.vector.tensor_tensor(k.b2[:], k.b2[:], t, ALU.add).then_inc(chain, 1)
            nc.vector.tensor_tensor(k.a2[:], k.a2[:], k.a1[:], ALU.mult).then_inc(chain, 1)
            dve.wait_ge(chain, 3)
            for row in (k.a1, k.b1):
                nc.vector.tensor_scalar(row[:], row[:], ALPHA, None, ALU.mult).then_inc(chain, 1)
            dve.wait_ge(chain, 5)


def out_projection(nc, k, w_hi, w_lo, lgP):
    with ExitStack() as ctx:
        sb, ps, sem = k.makers(ctx)
        HALF = YTILES // 2
        yraw = sb("yraw", [P, HALF, P])
        yhi = [sb(f"yhi{b}", [P, YTILES, P], F32R) for b in range(2)]
        ylo = [sb(f"ylo{b}", [P, YTILES, P], F32R) for b in range(2)]
        r, h2, h2t = sb("r", [P, D]), sb("h2", [P, D]), sb("h2t", [P, KK, P])
        wr = sb("w_router", [P, KK, EXPERTS])
        bst, mv, ve, nmr = sb("bst", [P, 2, 6]), sb("mv", [P, 2]), sb("ve", [P, 1]), sb("nmr", [P, 1])
        rstd = sb("rstd", [P, 1])
        op = [[ps(f"op{b}{n}", [P, 512]) for n in range(2)] for b in range(2)]
        tp = [ps(f"tp{n}", [P, 512]) for n in range(2)]
        (y_in, wr_in, hi_done, lo_done, o_mm, t_done, r_done, bn_done, mv_done, ve_done, rstd_done, nmr_done,
         xn_done, xa_out, ha_done, h2_done, h2_out, tr_done, ht_done, lg_mm, xm_done, xa_done) = (sem(n) for n in (
             "y_in wr_in yhi_done ylo_done o_mm t_done r_done bn_done mv_done ve_done rstd_done nmr_done "
             "xn_done xa_out ha_done h2_done h2_out trh_done ht_done lg_mm xm_done xa_done").split())
        x_in = sem("xo_in")
        block = ctx.enter_context(nc.Block())

        def loop(eng, step, extra=0):
            step(0, 0)
            step(1, 1)
            with eng.Fori(1, TT // 2 - 1) as h:
                step(2 * h, 0)
                step(2 * h + 1, 1)
            for i in range(TT - 2, TT + extra):
                step(i, i % 2)

        @block.sync
        def _(sp):
            sp.dma_start(wr[:], k.d["w_router"].rearrange("(kk p) e -> p kk e", p=P)).then_inc(wr_in, 16)

            def load_y(i, half):
                if half or in_loop(i, 1):
                    sp.wait_ge(lo_done, 2 * i + half)
                sp.dma_start(yraw[:], k.ytd[bass.ds(i, 1)].rearrange("a p m t -> (a p) m t")
                             [:, half * HALF:(half + 1) * HALF, :]).then_inc(y_in, 16)

            def step(i, b):
                if in_loop(i, 0, TT - 1):
                    load_y(i + 1, 0)
                if in_loop(i, 1):
                    sp.wait_ge(xa_out, 16 * i)
                sp.dma_start(r[:], k.d["x"].rearrange("(a p) n -> a p n", p=P)[bass.ds(i, 1)]
                             .rearrange("a p n -> (a p) n")).then_inc(x_in, 16)
                if in_loop(i, 0, TT - 1):
                    load_y(i + 1, 1)

            load_y(0, 0)
            load_y(0, 1)
            loop(sp, step)

        @block.gpsimd
        def _(pool):
            def step(i, b):
                pool.wait_ge(ve_done, i + 1)
                nc.gpsimd.tensor_tensor(rstd[:], ve[:], k.negh[:, 0:1], ALU.pow).then_inc(rstd_done, 1)
                pool.wait_ge(xn_done, i + 1)
                pool.wait_ge(ha_done, i + 1)
                nc.gpsimd.tensor_tensor(r[:], r[:], k.a1[:], ALU.mult).then_inc(xm_done, 1)
                pool.wait_ge(xm_done, i + 1)
                nc.gpsimd.tensor_tensor(r[:], r[:], k.b1[:], ALU.add).then_inc(xa_done, 1)

            loop(pool, step)

        @block.tensor
        def _(pe):
            def products(b, n):
                q = 0
                for yp, wp in ((yhi, w_hi), (yhi, w_lo), (ylo, w_hi)):
                    for m in range(YTILES):
                        mm = nc.tensor.matmul(op[b][n][:], yp[b][:, m, :], wp[:, m, n * 512:(n + 1) * 512],
                                              start=q == 0, stop=q == 3 * YTILES - 1)
                        q += 1
                mm.then_inc(o_mm, 1)

            def turn(j):
                pe.wait_ge(h2_done, j + 1)
                if in_loop(j, 1):
                    pe.wait_ge(ht_done, 2 * j)
                for n in range(2):
                    for q in range(4):
                        tr = nc.tensor.transpose(tp[n][:, q * P:(q + 1) * P],
                                                 h2[:, (4 * n + q) * P:(4 * n + q + 1) * P], k.ident[:])
                    tr.then_inc(tr_done, 1)

            def logits(j):
                pe.wait_ge(ht_done, 2 * (j + 1))
                if not in_loop(j, 1):
                    pe.wait_ge(wr_in, 16)
                for kk in range(KK):
                    mm = nc.tensor.matmul(lgP[:, bass.ds(j * EXPERTS, EXPERTS)], h2t[:, kk, :], wr[:, kk, :],
                                          start=kk == 0, stop=kk == KK - 1)
                mm.then_inc(lg_mm, 1)

            def step(i, b):
                here, before = in_loop(i, 0, TT), in_loop(i, 1, TT + 1)
                if here:
                    pe.wait_ge(lo_done, 2 * (i + 1))
                    if in_loop(i, 2):
                        pe.wait_ge(t_done, 2 * (i - 1))
                    products(b, 0)
                if before:
                    turn(i - 1)
                if here:
                    products(b, 1)
                if before:
                    logits(i - 1)

            loop(pe, step, 1)

        @block.scalar
        def _(act):
            def split(i, b):
                for half in range(2):
                    act.wait_ge(y_in, 16 * (2 * i + half + 1))
                    if half == 0 and in_loop(i, 2):
                        act.wait_ge(o_mm, 2 * (i - 1))
                    nc.scalar.copy(yhi[b][:, half * HALF:(half + 1) * HALF, :], yraw[:]).then_inc(hi_done, 1)

            def step(i, b):
                j = i - 1
                if in_loop(j, 0, TT):
                    act.wait_ge(nmr_done, j + 1)
                    nc.scalar.activation(r[:], r[:], ACT.Identity, bias=nmr[:], scale=rstd[:]).then_inc(xn_done, 1)
                    act.wait_ge(h2_done, j + 1)
                    if in_loop(j, 1, TT):
                        act.wait_ge(h2_out, 16 * j)
                    act.dma_start(k.h2d[bass.ds(j * P, P), :], h2[:]).then_inc(h2_out, 16)
                    if in_loop(j, 1, TT):
                        act.wait_ge(lg_mm, j)
                    for n in range(2):
                        act.wait_ge(tr_done, 2 * j + n + 1)
                        nc.scalar.copy(h2t[:, 4 * n:4 * n + 4, :].rearrange("p q t -> p (q t)"), tp[n][:]
                                       ).then_inc(ht_done, 1)
                    act.wait_ge(xa_done, j + 1)
                    act.dma_start(k.xad[bass.ds(j, 1)].rearrange("a p n -> (a p) n"), r[:]).then_inc(xa_out, 16)
                if in_loop(i, 0, TT - 1):
                    split(i + 1, 1 - b)

            split(0, 0)
            loop(act, step, 1)
            act.wait_ge(xa_out, 16 * TT)
            act.wait_ge(h2_out, 16 * TT)

        @block.vector
        def _(dve):
            def low(i, b):
                for half in range(2):
                    dve.wait_ge(hi_done, 2 * i + half + 1)
                    part = slice(half * HALF, (half + 1) * HALF)
                    nc.vector.tensor_tensor(ylo[b][:, part, :], yraw[:], yhi[b][:, part, :].bitcast(F32), ALU.subtract
                                            ).then_inc(lo_done, 1)

            def tile(j, jb):
                if in_loop(j, 1):
                    dve.wait_ge(tr_done, 2 * j)
                    dve.wait_ge(h2_out, 16 * j)
                for n in range(2):
                    dve.wait_ge(o_mm, 2 * j + n + 1)
                    nc.vector.tensor_tensor(h2[:, n * 512:(n + 1) * 512], op[jb][n][:],
                                            k.g1[:, n * 512:(n + 1) * 512], ALU.mult).then_inc(t_done, 1)
                dve.wait_ge(x_in, 16 * (j + 1))
                dve.wait_ge(t_done, 2 * (j + 1))
                nc.vector.scalar_tensor_tensor(out=r[:], in0=r[:], scalar=ALPHA, in1=h2[:], op0=ALU.mult,
                                               op1=ALU.add).then_inc(r_done, 1)
                dve.wait_ge(r_done, j + 1)
                for n in range(2):
                    nc.vector.bn_stats(bst[:, n, :], r[:, n * 512:(n + 1) * 512]).then_inc(bn_done, 1)
                dve.wait_ge(bn_done, 2 * (j + 1))
                dve.sem_inc(k.passed, 1)
                nc.vector.bn_aggr(mv[:], bst[:].rearrange("p a b -> p (a b)")).then_inc(mv_done, 1)
                dve.wait_ge(mv_done, j + 1)
                nc.vector.tensor_scalar(ve[:], mv[:, 1:2], EPS, None, ALU.add).then_inc(ve_done, 1)
                dve.wait_ge(rstd_done, j + 1)
                nc.vector.scalar_tensor_tensor(out=nmr[:], in0=mv[:, 0:1], scalar=-1.0, in1=rstd[:], op0=ALU.mult,
                                               op1=ALU.mult).then_inc(nmr_done, 1)
                dve.wait_ge(xn_done, j + 1)
                nc.vector.tensor_tensor(h2[:], r[:], k.a2[:], ALU.mult).then_inc(ha_done, 1)
                dve.wait_ge(ha_done, j + 1)
                nc.vector.tensor_tensor(h2[:], h2[:], k.b2[:], ALU.add).then_inc(h2_done, 1)

            def step(i, b):
                if in_loop(i, 1):
                    tile(i - 1, 1 - b)
                if in_loop(i, 0, TT - 1):
                    low(i + 1, 1 - b)

            low(0, 0)
            loop(dve, step, 1)


def route(nc, k, lgP):
    with ExitStack() as ctx:
        sb, ps, sem = k.makers(ctx)
        E, N = EXPERTS, TT * EXPERTS
        G4 = TT * EGROUPS
        rb = sb("rb", [P, E])
        p, eq, oh1, oh2, pm, cand = (sb(n, [P, N]) for n in "p eq oh1 oh2 pm cand".split())
        mx, sm = sb("mx", [P, TT]), sb("sm", [P, TT])
        m1, m2, i1, gs, gh = (sb(n, [P, G4]) for n in "m1 m2 i1 gs gh".split())
        off, cnt, base = sb("off", [P, TT + 1, E]), sb("cnt", [P, N]), sb("base", [P, E])
        nt, end = sb("nt", [P, E]), sb("end", [P, E])
        cmp = sb("cmp", [P, NTAB, E])
        ef = sb("ef", [P, NTAB])
        slf = sb("slf", [P, TT])
        zero = sb("zero", [NTAB, P])
        wa = [sb(f"wg2_{n}", [P, KK, 512]) for n in range(2)]
        csb = sb("csb2", [P, KK, P])
        gp = [ps(f"g2p{n}", [P, 512]) for n in range(2)]
        pre, cnp = ps("pre", [P, 512]), ps("cnp", [P, 512])
        chain, rb_in, exp_done, cnt_mm, zero_out, zset, slot_ready, g2_mm, g2_in, cs_wide = (sem(n) for n in (
            "chain_q rb_in exp_q cnt_mm zslot_out zset slot_ready g2_mm g2_in cs_wide2").split())
        wa_in = [sem(f"wg2_in{n}") for n in range(2)]
        block = ctx.enter_context(nc.Block())

        @block.sync
        def _(sp):
            sp.dma_start(rb[:], k.d["b_router"].partition_broadcast(P)).then_inc(rb_in, 16)
            sp.wait_ge(zset, 1)
            sp.dma_start(k.slotd.rearrange("(a b) c -> a (b c)", b=P), zero[:]).then_inc(zero_out, 16)
            w_ada = k.d["w_ada"].rearrange("(kk p) n -> p kk n", p=P)
            for n in range(2):
                sp.dma_start(wa[n][:], w_ada[:, :, 5 * D + n * 512:5 * D + (n + 1) * 512]).then_inc(wa_in[n], 16)
            sp.dma_start(k.g2[:], k.d["b_ada"][0, 5 * D:6 * D].partition_broadcast(P)).then_inc(g2_in, 16)
            sp.wait_ge(zero_out, 16)

        @block.gpsimd
        def _(pool):
            nc.gpsimd.memset(zero[:], 0.0).then_inc(zset, 1)

        @block.scalar
        def _(act):
            for kk in range(KK):
                nc.scalar.activation(csb[:, kk, :], k.ones[:], ACT.Copy, scale=k.cs[:, kk:kk + 1]).then_inc(cs_wide, 1)
            act.wait_ge(chain, 3)
            nc.scalar.activation(p[:], p[:], ACT.Exp).then_inc(exp_done, 1)

        @block.tensor
        def _(pe):
            pe.wait_ge(cs_wide, KK)
            for n in range(2):
                pe.wait_ge(wa_in[n], 16)
                for kk in range(KK):
                    mm = nc.tensor.matmul(gp[n][:], csb[:, kk, :], wa[n][:, kk, :], start=kk == 0, stop=kk == KK - 1)
                mm.then_inc(g2_mm, 1)
            pe.wait_ge(slot_ready, 1)
            nc.tensor.matmul(pre[:], k.below[:], eq[:], start=True, stop=True)
            nc.tensor.matmul(cnp[:], k.ones[:], eq[:], start=True, stop=True).then_inc(cnt_mm, 1)

        @block.vector
        def _(dve):
            count = [0]

            def link(ins):
                count[0] += 1
                ins.then_inc(chain, 1)
                dve.wait_ge(chain, count[0])

            v = nc.vector

            def over(ap, n, m):
                return ap.unsqueeze(2).to_broadcast([P, n, m])

            def along(ap, n, m):
                return ap.unsqueeze(1).to_broadcast([P, n, m])

            def rows(t, m):
                return t[:].rearrange("p (n m) -> p n m", m=m)

            dve.wait_ge(rb_in, 16)
            link(v.tensor_tensor(rows(p, E), lgP[:].rearrange("p (n m) -> p n m", m=E), along(rb[:], TT, E), ALU.add))
            link(v.tensor_reduce(mx[:], rows(p, E), AX.X, ALU.max))
            link(v.tensor_tensor(rows(p, E), rows(p, E), over(mx[:], TT, E), ALU.subtract))
            dve.wait_ge(exp_done, 1)
            link(v.tensor_reduce(sm[:], rows(p, E), AX.X, ALU.add))
            link(v.reciprocal(sm[:], sm[:]))
            link(v.tensor_tensor(rows(p, E), rows(p, E), over(sm[:], TT, E), ALU.mult))

            def first_max(values, m, n, w, idx, hot):
                link(v.tensor_reduce(m, values, AX.X, ALU.max))
                link(v.tensor_tensor(hot, values, over(m, n, w), ALU.is_equal))
                link(v.scalar_tensor_tensor(out=cand[:, 0:n * w].rearrange("p (n m) -> p n m", m=w), in0=hot,
                                            scalar=-float(EPG), in1=along(k.eidx[:, 0:w], n, w), op0=ALU.mult,
                                            op1=ALU.add))
                link(v.tensor_reduce(idx, cand[:, 0:n * w].rearrange("p (n m) -> p n m", m=w), AX.X, ALU.min))
                link(v.tensor_scalar(idx, idx, float(EPG), None, ALU.add))
                link(v.tensor_tensor(hot, along(k.eidx[:, 0:w], n, w), over(idx, n, w), ALU.is_equal))

            first_max(rows(p, EPG), m1[:], G4, EPG, i1[:], rows(oh1, EPG))
            link(v.scalar_tensor_tensor(out=pm[:], in0=oh1[:], scalar=-4.0, in1=p[:], op0=ALU.mult, op1=ALU.add))
            first_max(rows(pm, EPG), m2[:], G4, EPG, i1[:], rows(oh2, EPG))
            link(v.tensor_tensor(gs[:], m1[:], m2[:], ALU.add))
            first_max(rows(gs, EGROUPS), mx[:], TT, EGROUPS, sm[:], rows(gh, EGROUPS))
            for oh in (oh1, oh2):
                link(v.tensor_tensor(rows(oh, EPG), rows(oh, EPG), over(gh[:], G4, EPG), ALU.mult))
            for m, g in ((m1, k.gate_a), (m2, k.gate_b)):
                link(v.tensor_tensor(m[:], m[:], gh[:], ALU.mult))
                link(v.tensor_reduce(g[:], rows(m, EGROUPS), AX.X, ALU.add))
            link(v.tensor_tensor(sm[:], k.gate_a[:], k.gate_b[:], ALU.add))
            link(v.reciprocal(sm[:], sm[:]))
            for g in (k.gate_a, k.gate_b):
                link(v.tensor_tensor(g[:], g[:], sm[:], ALU.mult))
            v.tensor_tensor(eq[:], oh1[:], oh2[:], ALU.add).then_inc(slot_ready, 1)
            dve.wait_ge(g2_in, 16)
            for n in range(2):
                dve.wait_ge(g2_mm, n + 1)
                half = k.g2[:, n * 512:(n + 1) * 512]
                link(v.scalar_tensor_tensor(out=half, in0=gp[n][:], scalar=1.0, in1=half, op0=ALU.add, op1=ALU.add))
            dve.wait_ge(cnt_mm, 1)
            link(v.tensor_copy(cnt[:], cnp[:]))
            link(v.memset(off[:, 0, :], 0.0))
            for t in range(TT):
                link(v.tensor_tensor(off[:, t + 1, :], off[:, t, :], cnt[:, t * E:(t + 1) * E], ALU.add))
            link(v.tensor_scalar(ef[:], k.tidx[:], float(P), None, ALU.mult))
            link(v.tensor_tensor(cmp[:, 0:TT, :].rearrange("p a b -> p (a b)").rearrange("p (e j) -> p e j", j=TT),
                                 over(off[:, TT, :], E, TT), along(ef[:, 0:TT], E, TT), ALU.is_gt))
            link(v.tensor_reduce(nt[:], cmp[:, 0:TT, :].rearrange("p a b -> p (a b)").rearrange("p (e j) -> p e j", j=TT),
                                 AX.X, ALU.add))
            link(v.tensor_tensor_scan(end[:], k.ones[:, 0:E], nt[:], 0.0, ALU.mult, ALU.add))
            link(v.tensor_tensor(base[:], end[:], nt[:], ALU.subtract))
            link(v.tensor_scalar(base[:], base[:], float(P), None, ALU.mult))
            link(v.tensor_tensor(cand[:], pre[:], off[:, 0:TT, :].rearrange("p a b -> p (a b)"), ALU.add))
            link(v.tensor_tensor(rows(cand, E), rows(cand, E), along(base[:], TT, E), ALU.add))
            for oh, slots in ((oh1, k.slot_a), (oh2, k.slot_b)):
                link(v.tensor_tensor(pm[:], cand[:], oh[:], ALU.mult))
                link(v.tensor_reduce(slf[:], rows(pm, E), AX.X, ALU.add))
                link(v.tensor_copy(slots[:], slf[:]))
            link(v.tensor_tensor(cmp[:], along(end[:], NTAB, E), over(k.tidx[:], NTAB, E), ALU.is_le))
            link(v.tensor_reduce(ef[:], cmp[:], AX.X, ALU.add))
            link(v.tensor_scalar(ef[:], ef[:], float(E - 1), None, ALU.min))
            link(v.tensor_copy(k.tile_expert[:], ef[:]))
            link(v.memset(k.fresh[:], 1))
            link(v.tensor_tensor(k.fresh[:, 1:NTAB], ef[:, 1:NTAB], ef[:, 0:NTAB - 1], ALU.not_equal))
            link(v.tensor_scalar(ef[:, 0:MAXT // 2], k.tidx[:, 0:MAXT // 2], 2.0, None, ALU.mult))
            link(v.tensor_scalar(cmp[:, 0, :], ef[:, 0:MAXT // 2], end[:, E - 1:E], None, ALU.is_lt))
            link(v.tensor_reduce(sm[:, 0:1], cmp[:, 0, :], AX.X, ALU.add))
            link(v.tensor_scalar(k.last_pair[:], sm[:, 0:1], -1.0, None, ALU.add))


def experts(nc, k):
    with ExitStack() as ctx:
        sb, ps, sem = k.makers(ctx)
        FQ = FE // P
        GU = 4
        PIECES = GU + 2
        raw = [sb(f"piece_raw{q}", [P, 4, 512]) for q in range(PIECES)]
        hi = [sb(f"piece_hi{q}", [P, 4, 512], F32R) for q in range(PIECES)]
        lo = [sb(f"piece_lo{q}", [P, 4, 512], F32R) for q in range(PIECES)]
        ix = [sb(f"ix{b}", [P, 1], I32) for b in range(2)]
        xg = [sb(f"xg{b}", [P, D]) for b in range(2)]
        xt_hi, xt_lo = sb("xt_hi", [P, KK, P], F32R), sb("xt_lo", [P, KK, P], F32R)
        ht_hi, ht_lo = sb("ht_hi", [P, FQ, P], F32R), sb("ht_lo", [P, FQ, P], F32R)
        th, a, h = sb("th_e", [P, FE]), sb("a_e", [P, FE]), sb("h_e", [P, FE])
        ye = [sb(f"ye{b}", [P, D]) for b in range(2)]
        xp = [ps(f"xp{n}", [P, 512]) for n in range(2)]
        gp, up, hp = ps("gp_e", [P, 512]), ps("up_e", [P, 512]), ps("hp_e", [P, 512])
        yp = [ps(f"yp{n}", [P, 512]) for n in range(2)]
        idr = sb("idr", [NTAB, P])
        scat, id_in, id_tr, ids_ready = (sem(n) for n in "scat id_in id_tr ids_ready".split())
        loaded = [sem(f"w_loaded{q}") for q in range(PIECES)]
        hi_done = [sem(f"w_hi_done{q}") for q in range(PIECES)]
        lo_done = [sem(f"w_lo_done{q}") for q in range(PIECES)]
        used = [sem(f"w_used{q}") for q in range(PIECES)]
        x_in = [sem(f"xg_in{b}") for b in range(2)]
        ye_out = [sem(f"ye_out{b}") for b in range(2)]
        (ix_ready, x_tr, xt_hi_done, xt_lo_done, th_done, a_done, h_done, h_tr, ht_hi_done, ht_lo_done, ye_done) = (
            sem(n) for n in ("ix_ready x_tr xt_hi_done xt_lo_done the_done a_done h_done h_tr ht_hi_done ht_lo_done "
                             "ye_done").split())
        block = ctx.enter_context(nc.Block())

        def loop(eng, step):
            last = eng.value_load(k.last_pair[0:1, 0:1], min_val=TT - 1, max_val=MAXT // 2 - 1)
            step(0, 0)
            step(1, 1)
            with eng.Fori(1, last + 1) as q:
                step(2 * q, 0)
                step(2 * q + 1, 1)
            return last

        @block.sync
        def _(sp):
            def load(t, pieces):
                e = sp.value_load(k.tile_expert[0:1, bass.ds(t, 1)], min_val=0, max_val=EXPERTS - 1)
                fresh = sp.value_load(k.fresh[0:1, bass.ds(t, 1)], min_val=0, max_val=1)
                for q in pieces:
                    if q < GU:
                        w = k.d["w_gate" if q < 2 else "w_up"][bass.ds(e, 1)]
                        w = w.rearrange("e (kk p) f -> p (e kk) f", p=P)[:, (q % 2) * 4:(q % 2) * 4 + 4, :]
                    else:
                        w = k.d["w_down"][bass.ds(e, 1)]
                        w = w.rearrange("e (kk p) f -> p (e kk) f", p=P)[:, :, (q - GU) * 512:(q - GU + 1) * 512]
                    if in_loop(t, 1):
                        sp.wait_ge(lo_done[q], t)
                    sp.dma_start(raw[q][:], w, cond=fresh > 0).then_inc(loaded[q], 16)

            def step(t, b):
                load(t + 1, range(GU))
                load(t, range(GU, PIECES))

            load(0, range(GU))
            sp.wait_ge(scat, 16 * 2 * TT)
            sp.dma_start(idr[:], k.slotd.rearrange("(a b) c -> a (b c)", b=P)).then_inc(id_in, 16)
            loop(sp, step)

        def low_part(eng, v, q, t):
            if in_loop(t, 1):
                eng.wait_ge(used[q], t)
            eng.wait_ge(hi_done[q], t + 1)
            v.tensor_tensor(lo[q][:], raw[q][:], hi[q][:].bitcast(F32), ALU.subtract).then_inc(lo_done[q], 1)

        @block.gpsimd
        def _(pool):
            def fetch(t, b):
                if in_loop(t, 2):
                    pool.wait_ge(x_tr, 2 * (t - 1))
                    pool.sem_inc(k.passed, 1)
                nc.gpsimd.tensor_copy(ix[b][:], k.ids[:, bass.ds(t, 1)]).then_inc(ix_ready, 1)
                pool.wait_ge(ix_ready, t + 1)
                pool.sem_inc(k.passed, 1)
                nc.gpsimd.indirect_dma_start(out=xg[b][:], out_offset=None, in_=k.h2d[:],
                                             in_offset=bass.IndirectOffsetOnAxis(ap=ix[b][:], axis=0)
                                             ).then_inc(x_in[b], 16)

            def step(t, b):
                fetch(t + 2, b)
                low_part(pool, nc.gpsimd, 3, t + 1)
                low_part(pool, nc.gpsimd, 5, t)

            for i in range(TT):
                for slots in (k.slot_a, k.slot_b):
                    nc.gpsimd.indirect_dma_start(
                        out=k.slotd[:], out_offset=bass.IndirectOffsetOnAxis(ap=slots[:, i:i + 1], axis=0),
                        in_=k.tok[:, i:i + 1], in_offset=None).then_inc(scat, 16)
            pool.wait_ge(scat, 16 * 2 * TT)
            pool.wait_ge(ids_ready, 1)
            pool.sem_inc(k.passed, 1)
            fetch(0, 0)
            fetch(1, 1)
            low_part(pool, nc.gpsimd, 3, 0)
            last = loop(pool, step)
            for b in range(2):
                pool.wait_ge(x_in[b], 16 * (last + 2))
                pool.sem_inc(k.passed, 1)

        @block.tensor
        def _(pe):
            def turn(t, b):
                pe.wait_ge(x_in[b], 16 * (t // 2 + 1))
                if in_loop(t, 1):
                    pe.wait_ge(xt_lo_done, 2 * t)
                for n in range(2):
                    for q in range(4):
                        tr = nc.tensor.transpose(xp[n][:, q * P:(q + 1) * P],
                                                 xg[b][:, (4 * n + q) * P:(4 * n + q + 1) * P], k.ident[:])
                    tr.then_inc(x_tr, 1)

            def products(acc, l_hi, l_lo, first, q, start, stop):
                for kk in range(4):
                    for n, (l, r) in enumerate(((l_hi, lo[q]), (l_hi, hi[q]), (l_lo, hi[q]))):
                        mm = nc.tensor.matmul(acc[:], l[:, first + kk, :], r[:, kk, :], start=start and kk == 0 and n == 0,
                                              stop=stop and kk == 3 and n == 2)
                mm.then_inc(used[q], 1)

            def down(t):
                pe.wait_ge(ht_lo_done, t + 1)
                for n in range(2):
                    pe.wait_ge(lo_done[GU + n], t + 1)
                    if n == 0 and not in_loop(t, 1):
                        pe.wait_ge(ids_ready, 1)
                    if in_loop(t, 1):
                        pe.wait_ge(ye_done, 2 * t + n - 1)
                    products(yp[n], ht_hi, ht_lo, 0, GU + n, True, True)

            def step(t, b):
                pe.wait_ge(xt_lo_done, 2 * (t + 1))
                if in_loop(t, 1):
                    pe.wait_ge(h_done, t)
                for q in range(GU):
                    pe.wait_ge(lo_done[q], t + 1)
                    products(gp if q < 2 else up, xt_hi, xt_lo, 4 * (q % 2), q, q % 2 == 0, q % 2 == 1)
                turn(t + 1, 1 - b)
                if in_loop(t, 1):
                    down(t - 1)
                pe.wait_ge(h_done, t + 1)
                if in_loop(t, 1):
                    pe.wait_ge(ht_lo_done, t)
                for q in range(FQ):
                    tr = nc.tensor.transpose(hp[:, q * P:(q + 1) * P], h[:, q * P:(q + 1) * P], k.ident[:])
                tr.then_inc(h_tr, 1)

            pe.wait_ge(id_in, 16)
            nc.tensor.transpose(yp[0][:, 0:NTAB], idr[:], k.ident[0:NTAB, 0:NTAB]).then_inc(id_tr, 1)
            turn(0, 0)
            last = loop(pe, step)
            down(2 * last + 1)

        @block.scalar
        def _(act):
            def high_part(q, t):
                act.wait_ge(loaded[q], 16 * (t + 1))
                if in_loop(t, 1):
                    act.wait_ge(used[q], t)
                nc.scalar.copy(hi[q][:], raw[q][:]).then_inc(hi_done[q], 1)

            def xt_high(t):
                for n in range(2):
                    act.wait_ge(x_tr, 2 * t + n + 1)
                    if n == 0 and in_loop(t, 1):
                        act.wait_ge(used[GU - 1], t)
                    nc.scalar.copy(xt_hi[:, 4 * n:4 * n + 4, :].rearrange("p q t -> p (q t)"), xp[n][:]
                                   ).then_inc(xt_hi_done, 1)

            def store(t, b):
                act.wait_ge(ye_done, 2 * (t + 1))
                act.dma_start(k.ysd[bass.ds(t * P, P), :], ye[b][:]).then_inc(ye_out[b], 16)

            def step(t, b):
                high_part(0, t + 1)
                act.wait_ge(used[1], t + 1)
                if in_loop(t, 1):
                    act.wait_ge(a_done, t)
                nc.scalar.activation(th[:], gp[:], ACT.Tanh, scale=0.5).then_inc(th_done, 1)
                for q in range(1, GU):
                    high_part(q, t + 1)
                xt_high(t + 1)
                high_part(GU, t)
                act.wait_ge(h_tr, t + 1)
                if in_loop(t, 1):
                    act.wait_ge(used[PIECES - 1], t)
                nc.scalar.activation(ht_hi[:].rearrange("p q t -> p (q t)"), hp[:], ACT.Copy, scale=0.5
                                     ).then_inc(ht_hi_done, 1)
                high_part(GU + 1, t)
                if in_loop(t, 1):
                    store(t - 1, 1 - b)

            for q in range(GU):
                high_part(q, 0)
            xt_high(0)
            last = loop(act, step)
            store(2 * last + 1, 1)
            for b in range(2):
                act.wait_ge(ye_out[b], 16 * (last + 1))
                act.sem_inc(k.passed, 1)

        @block.vector
        def _(dve):
            def xt_low(t):
                for n in range(2):
                    dve.wait_ge(xt_hi_done, 2 * t + n + 1)
                    if n == 0 and in_loop(t, 1):
                        dve.wait_ge(used[GU - 1], t)
                    part = [v[:, 4 * n:4 * n + 4, :].rearrange("p q t -> p (q t)") for v in (xt_lo, xt_hi)]
                    nc.vector.tensor_tensor(part[0], xp[n][:], part[1].bitcast(F32), ALU.subtract
                                            ).then_inc(xt_lo_done, 1)

            def result(t, b, n):
                if n == 0 and in_loop(t, 2):
                    dve.wait_ge(ye_out[b], 16 * (t // 2))
                dve.wait_ge(used[GU + n], t + 1)
                nc.vector.tensor_tensor(ye[b][:, n * 512:(n + 1) * 512], yp[n][:], k.g2[:, n * 512:(n + 1) * 512],
                                        ALU.mult).then_inc(ye_done, 1)

            def step(t, b):
                low_part(dve, nc.vector, 0, t + 1)
                dve.wait_ge(th_done, t + 1)
                if in_loop(t, 1):
                    dve.wait_ge(h_done, t)
                nc.vector.scalar_tensor_tensor(out=a[:], in0=th[:], scalar=1.0, in1=gp[:], op0=ALU.add,
                                               op1=ALU.mult).then_inc(a_done, 1)
                low_part(dve, nc.vector, 1, t + 1)
                low_part(dve, nc.vector, 2, t + 1)
                dve.wait_ge(a_done, t + 1)
                dve.wait_ge(used[GU - 1], t + 1)
                if in_loop(t, 1):
                    dve.wait_ge(h_tr, t)
                nc.vector.tensor_tensor(h[:], a[:], up[:], ALU.mult).then_inc(h_done, 1)
                xt_low(t + 1)
                if in_loop(t, 1):
                    result(t - 1, 1 - b, 0)
                low_part(dve, nc.vector, GU, t)
                if in_loop(t, 1):
                    result(t - 1, 1 - b, 1)
                dve.wait_ge(ht_hi_done, t + 1)
                if in_loop(t, 1):
                    dve.wait_ge(used[PIECES - 1], t)
                nc.vector.scalar_tensor_tensor(out=ht_lo[:].rearrange("p q t -> p (q t)"), in0=hp[:], scalar=0.5,
                                               in1=ht_hi[:].rearrange("p q t -> p (q t)").bitcast(F32),
                                               op0=ALU.mult, op1=ALU.subtract).then_inc(ht_lo_done, 1)

            for q in range(3):
                low_part(dve, nc.vector, q, 0)
            dve.wait_ge(id_tr, 1)
            nc.vector.tensor_copy(k.ids[:], yp[0][:, 0:NTAB]).then_inc(ids_ready, 1)
            xt_low(0)
            last = loop(dve, step)
            for n in range(2):
                result(2 * last + 1, 1, n)


def output(nc, k, out):
    with ExitStack() as ctx:
        sb, ps, sem = k.makers(ctx)
        R = 4
        lng, lnb = (sb(n, [P, D]) for n in "lng2 lnb2".split())
        ia, ib = [sb(f"ia{s}", [P, 1], I32) for s in range(R)], [sb(f"ib{s}", [P, 1], I32) for s in range(R)]
        ga, gb = [sb(f"ga{s}", [P, 1]) for s in range(R)], [sb(f"gb{s}", [P, 1]) for s in range(R)]
        ya, yb = [sb(f"ya{s}", [P, D]) for s in range(R)], [sb(f"yb{s}", [P, D]) for s in range(R)]
        xa = [sb(f"xa{s}", [P, D]) for s in range(R)]
        m, r, o = ([sb(f"{n}{b}", [P, D]) for b in range(2)] for n in ("m_", "r_", "o_"))
        bst, mv, ve, nmr = sb("bst2", [P, 2, 6]), sb("mv2", [P, 2]), sb("ve2", [P, 1]), sb("nmr2", [P, 1])
        rstd = sb("rstd2", [P, 1])
        (row_in, cols, mg_done, ms_done, r_done, bn_done, mv_done, ve_done,
         rstd_done, nmr_done, n_done, og_done, o_done) = (sem(n) for n in (
             "row_in cols mg_done msum_done r2_done bn2 mv2s ve2s rstd2s nmr2s "
             "n_done og_done o_done").split())
        ya_in, yb_in, xa_in = ([sem(f"{n}{s}") for s in range(R)] for n in ("ya_in", "yb_in", "xa_in"))
        stored = [sem(f"stored{b}") for b in range(2)]
        block = ctx.enter_context(nc.Block())

        def loop(eng, step, extra=0):
            for i in range(R):
                step(i, i)
            with eng.Fori(1, TT // R - 1) as q:
                for s in range(R):
                    step(R * q + s, s)
            for i in range(TT - R, TT + extra):
                step(i, i % R)

        @block.sync
        def _(sp):
            for row, src in ((lng, k.d["ln_g"][1]), (lnb, k.d["ln_b"][1])):
                sp.dma_start(row[:], src.partition_broadcast(P)).then_inc(row_in, 16)

            def load(i, s):
                if in_loop(i, R):
                    sp.wait_ge(r_done, i - R + 1)
                sp.dma_start(xa[s][:], k.xad[bass.ds(i, 1)].rearrange("a p n -> (a p) n")).then_inc(xa_in[s], 16)

            def step(i, s):
                if in_loop(i, 1):
                    sp.wait_ge(o_done, i)
                    b = (s - 1) % 2
                    sp.dma_start(out[bass.ds((i - 1) * P, P), :], o[b][:]).then_inc(stored[b], 16)
                if in_loop(i, 0, TT - R + 1):
                    load(i + R - 1, (s + R - 1) % R)

            for i in range(R - 1):
                load(i, i)
            loop(sp, step, 1)
            for b in range(2):
                sp.wait_ge(stored[b], 16 * TT // 2)

        @block.gpsimd
        def _(pool):
            def fetch(i, s):
                if in_loop(i, R):
                    pool.wait_ge(ms_done, i - R + 1)
                    pool.sem_inc(k.passed, 1)
                for dst, src in ((ia, k.slot_a), (ib, k.slot_b), (ga, k.gate_a), (gb, k.gate_b)):
                    nc.gpsimd.tensor_copy(dst[s][:], src[:, bass.ds(i, 1)]).then_inc(cols, 1)
                pool.wait_ge(cols, 4 * (i + 1))
                pool.sem_inc(k.passed, 1)
                for idx, y, arrived in ((ia, ya, ya_in), (ib, yb, yb_in)):
                    nc.gpsimd.indirect_dma_start(out=y[s][:], out_offset=None, in_=k.ysd[:],
                                                 in_offset=bass.IndirectOffsetOnAxis(ap=idx[s][:], axis=0)
                                                 ).then_inc(arrived[s], 16)

            def step(i, s):
                if in_loop(i, 1):
                    pool.wait_ge(ve_done, i)
                    if in_loop(i, 2):
                        pool.wait_ge(n_done, i - 1)
                    nc.gpsimd.tensor_tensor(rstd[:], ve[:], k.negh[:, 0:1], ALU.pow).then_inc(rstd_done, 1)
                if in_loop(i, 0, TT - R + 1):
                    fetch(i + R - 1, (s + R - 1) % R)

            for i in range(R - 1):
                fetch(i, i)
            loop(pool, step, 1)

        @block.scalar
        def _(act):
            def step(i, s):
                b = s % 2
                if in_loop(i, 0, TT):
                    act.wait_ge(ya_in[s], 16 * (i // R + 1))
                    act.wait_ge(cols, 4 * (i + 1))
                    if in_loop(i, 2):
                        act.wait_ge(r_done, i - 1)
                    nc.scalar.activation(m[b][:], ya[s][:], ACT.Copy, scale=ga[s][:]).then_inc(mg_done, 1)
                if in_loop(i, 1):
                    act.wait_ge(nmr_done, i)
                    nc.scalar.activation(r[1 - b][:], r[1 - b][:], ACT.Identity, bias=nmr[:], scale=rstd[:]
                                         ).then_inc(n_done, 1)

            loop(act, step, 1)

        @block.vector
        def _(dve):
            dve.wait_ge(row_in, 32)

            def step(i, s):
                b = s % 2
                if in_loop(i, 0, TT):
                    dve.wait_ge(mg_done, i + 1)
                    dve.wait_ge(yb_in[s], 16 * (i // R + 1))
                    nc.vector.scalar_tensor_tensor(out=m[b][:], in0=yb[s][:], scalar=gb[s][:], in1=m[b][:],
                                                   op0=ALU.mult, op1=ALU.add).then_inc(ms_done, 1)
                if in_loop(i, 1):
                    dve.wait_ge(rstd_done, i)
                    if in_loop(i, 2):
                        dve.wait_ge(n_done, i - 1)
                    nc.vector.scalar_tensor_tensor(out=nmr[:], in0=mv[:, 0:1], scalar=-1.0, in1=rstd[:],
                                                   op0=ALU.mult, op1=ALU.mult).then_inc(nmr_done, 1)
                if in_loop(i, 0, TT):
                    dve.wait_ge(ms_done, i + 1)
                    dve.wait_ge(xa_in[s], 16 * (i // R + 1))
                    if in_loop(i, 2):
                        dve.wait_ge(og_done, i - 1)
                    nc.vector.tensor_tensor(r[b][:], m[b][:], xa[s][:], ALU.add).then_inc(r_done, 1)
                    dve.wait_ge(r_done, i + 1)
                    if in_loop(i, 1):
                        dve.wait_ge(mv_done, i)
                    for n in range(2):
                        nc.vector.bn_stats(bst[:, n, :], r[b][:, n * 512:(n + 1) * 512]).then_inc(bn_done, 1)
                    dve.wait_ge(bn_done, 2 * (i + 1))
                    if in_loop(i, 1):
                        dve.wait_ge(nmr_done, i)
                    dve.sem_inc(k.passed, 1)
                    nc.vector.bn_aggr(mv[:], bst[:].rearrange("p a b -> p (a b)")).then_inc(mv_done, 1)
                    dve.wait_ge(mv_done, i + 1)
                    nc.vector.tensor_scalar(ve[:], mv[:, 1:2], EPS, None, ALU.add).then_inc(ve_done, 1)
                if in_loop(i, 1):
                    dve.wait_ge(n_done, i)
                    if in_loop(i, 3):
                        dve.wait_ge(stored[1 - b], 16 * ((i - 1) // 2))
                    nc.vector.tensor_tensor(o[1 - b][:], r[1 - b][:], lng[:], ALU.mult).then_inc(og_done, 1)
                    dve.wait_ge(og_done, i)
                    nc.vector.tensor_tensor(o[1 - b][:], o[1 - b][:], lnb[:], ALU.add).then_inc(o_done, 1)

            loop(dve, step, 1)


class Kit:

    def __init__(self, nc, d, ctx):
        self.nc, self.d, self.ctx = nc, d, ctx
        self.used, self.semaphores = [], ctx

        def scratch(name, shape, dt=F32):
            return nc.dram_tensor(name, shape, dt, kind="Internal").ap()

        self.hmd = scratch("hm_parts", (NC_, P, 2 * KK * CHUNK))
        self.acd = scratch("acum_rows", (STEPS * 2 * RH, P))
        self.ytd = scratch("y_t", (TT, P, YTILES, P))
        self.xad = scratch("alpha_x1", (TT, P, D))
        self.h2d = scratch("hm2", (SEQ, D))
        self.slotd = scratch("token_by_slot", (NTAB * P, 1))
        self.ysd = scratch("expert_out", (MAXT * P, D))
        sb, _, sem = self.makers(ctx)
        self.ident = sb("ident", [P, P])
        self.ones = sb("ones", [P, P])
        self.mask3 = sb("mask3", [P, 3 * P])
        self.below = sb("below", [P, P])
        self.keep = sb("keep", [P, STEPS + 2])
        self.negh = sb("negh", [P, 2])
        self.eps = sb("eps", [P, 2])
        self.eidx = sb("eidx", [P, EPG])
        self.tidx = sb("tidx", [P, NTAB])
        self.tok = sb("tok", [P, TT])
        self.eidx_i = sb("eidx_i", [P, EPG], I32)
        self.tidx_i = sb("tidx_i", [P, NTAB], I32)
        self.tok_i = sb("tok_i", [P, TT], I32)
        self.cs = sb("cs", [P, KK])
        self.par = sb("par", [P, GROUPS, CONV * (TAPS + 1)])
        self.drow = sb("drow", [P, HEADS])
        self.const_set = sem("const_set")
        self.passed = sem("passed")

    def later(self):
        sb, _, _ = self.makers(self.ctx)
        self.g2 = sb("g2", [P, D])
        self.gate_a, self.gate_b = sb("gate_a", [P, TT]), sb("gate_b", [P, TT])
        self.slot_a, self.slot_b = sb("slot_a", [P, TT], I32), sb("slot_b", [P, TT], I32)
        self.tile_expert = sb("tile_expert", [P, NTAB], I32)
        self.fresh = sb("fresh", [P, NTAB], I32)
        self.last_pair = sb("last_pair", [P, 1], I32)
        self.ids = sb("ids", [P, NTAB], I32)

    def makers(self, ctx):
        nc = self.nc
        return (lambda name, shape, dt=F32: ctx.enter_context(nc.sbuf_tensor(name, shape, dt)),
                lambda name, shape: ctx.enter_context(nc.psum_tensor(name, shape, F32)),
                self.semaphore)

    def semaphore(self, name):
        self.used.append(self.semaphores.enter_context(self.nc.semaphore(name)))
        return self.used[-1]


def program(nc, d, out):
    with ExitStack() as whole:
        k = Kit(nc, d, whole)
        with ExitStack() as ctx:
            constants(nc, k, ctx)
        with ExitStack() as ctx:
            sb, _, _ = k.makers(ctx)
            k.nwrow = sb("nwrow", [P, DI])
            k.tab = sb("tab", [P, 3, STEPS * 2 * RH])
            stage(nc, k, modulated_input)
            stage(nc, k, mixer_steps)
        k.later()
        with ExitStack() as ctx:
            _, ps, _ = k.makers(ctx)
            lgP = ps("lgP", [P, TT * EXPERTS])
            with ExitStack() as projection:
                sb, _, _ = k.makers(projection)
                k.g1, k.a1, k.b1, k.a2, k.b2 = (sb(n, [P, D]) for n in "g1 a1 b1 a2 b2".split())
                w_hi, w_lo = sb("wo_hi", [P, YTILES, D], F32R), sb("wo_lo", [P, YTILES, D], F32R)
                stage(nc, k, row_vectors, w_hi, w_lo)
                stage(nc, k, out_projection, w_hi, w_lo, lgP)
            stage(nc, k, route, lgP)
        stage(nc, k, experts)
        stage(nc, k, output, out)


def laid_out(inputs):
    import numpy as np
    a = {n: np.asarray(v) for n, v in inputs.items()}
    cw, cb = a["ssm_conv_w"][0], a["ssm_conv_b"][0]
    wb = np.concatenate([cw, cb[None]], 0)
    xs = wb[:, :DI].reshape(5, GROUPS, 2, P)
    bs = wb[:, DI:DI + GROUPS * STATE].reshape(5, GROUPS, 1, P)
    cc = wb[:, DI + GROUPS * STATE:].reshape(5, GROUPS, 1, P)
    par = np.concatenate([xs, bs, cc], 2).transpose(3, 1, 2, 0).reshape(P, GROUPS, CONV * 5)
    r = {
        "x": a["x"][0], "c_cols": a["c"].reshape(KK, P).T, "w_ada": a["w_ada"][0],
        "b_ada_cols": a["b_ada"][0, :2 * D].reshape(16, P).T, "b_ada": a["b_ada"],
        "ln_g": a["ln_g"][0], "ln_b": a["ln_b"][0], "w_in": a["ssm_w_in"][0], "conv_par": par,
        "dt_bias": a["ssm_dt_bias"][0], "a_log": a["ssm_a_log"][0], "d_skip": a["ssm_d"][0],
        "norm_w": a["ssm_norm_w"][0], "w_out": a["ssm_w_out"][0], "w_router": a["w_router"],
        "b_router": a["b_router"], "w_gate": a["moe_w_gate"][0], "w_up": a["moe_w_up"][0],
        "w_down": a["moe_w_down"][0],
    }
    return {n: np.ascontiguousarray(v) for n, v in r.items()}


def kernel(**inputs):
    import numpy as _np
    import concourse.bacc as _bacc
    from concourse.bass_utils import run_bass_kernel_spmd as _run

    nc = _bacc.Bacc("TRN2", target_bir_lowering=False, num_devices=1)
    arrays, d = {}, {}
    for name, a in laid_out(inputs).items():
        arrays[f"in_{name}"] = a
        d[name] = nc.dram_tensor(f"in_{name}", a.shape, mybir.dt.from_np(a.dtype), kind="ExternalInput").ap()
    out = nc.dram_tensor("out", (SEQ, D), F32, kind="ExternalOutput").ap()
    program(nc, d, out)
    r = _run(nc, [arrays], core_ids=[0])
    return _np.asarray(r.results[0]["out"]).reshape(1, SEQ, D)
```
